# Optimizing a Trainium2 kernel written in Bass

```python
import jax, jax.numpy as jnp
from jax import lax
import numpy as np

D_MODEL = 1024
BATCH = 1
SEQ = 256
DEPTH = 1
DEC_BATCH = 1
DEC_SEQ = 1024
PAST_LEN = 128

N_META = 16
D_MIX = D_MODEL
D_POOL = D_MIX // 4
POOL_WINDOWS = (2, 4, 8, 16)
N_POOL_GROUPS = len(POOL_WINDOWS)
D_POOL_GROUP = D_POOL // N_POOL_GROUPS
D_MLSTM = D_MIX - D_POOL
N_HEADS = 4
HEAD_DIM = D_MLSTM // N_HEADS
CHUNK = 64
CONV_K = 3
N_GATE = 4 * N_HEADS
N_IN = D_POOL + 4 * D_MLSTM + N_GATE
N_EXPERTS = 16
CAPACITY_FACTOR = 2
D_FF = D_MODEL
EPS = 1e-6
NEG = -1e30

kernel_name = "hybrid_pool_mlstm_ec_encoder"

def rmsnorm(x, g):
    xf = x.astype(jnp.float32)
    y = xf * lax.rsqrt(jnp.mean(xf * xf, axis=-1, keepdims=True) + EPS)
    return (y * g.astype(jnp.float32)).astype(x.dtype)

def pool_mixer(u, pool_w, pool_scale):
    B, L, _ = u.shape
    cs = jnp.cumsum(u.astype(jnp.float32), axis=1)
    cs = jnp.concatenate([jnp.zeros((B, 1, D_POOL), jnp.float32), cs], axis=1)
    t = np.arange(L)
    outs = []
    for gi, w in enumerate(POOL_WINDOWS):
        lo = np.clip(t - w // 2, 0, L)
        hi = np.clip(t - w // 2 + w, 0, L)
        cnt = (hi - lo).astype(np.float32)[None, :, None]
        sl = slice(gi * D_POOL_GROUP, (gi + 1) * D_POOL_GROUP)
        csg = cs[:, :, sl]
        mean = (csg[:, hi] - csg[:, lo]) / cnt
        mixed = (mean - u[:, :, sl].astype(jnp.float32)).astype(u.dtype)
        outs.append(jnp.einsum('blc,cd->bld', mixed, pool_w[gi]))
    return jnp.concatenate(outs, axis=-1) * pool_scale

def mlstm_chunkwise(q, k, v, logi, logf):
    B, H, Lp, DH = q.shape
    NC = Lp // CHUNK
    f32 = jnp.float32
    qc = q.reshape(B, H, NC, CHUNK, DH).astype(f32) * (DH ** -0.5)
    kc = k.reshape(B, H, NC, CHUNK, DH).astype(f32)
    vc = v.reshape(B, H, NC, CHUNK, DH).astype(f32)
    li = logi.reshape(B, H, NC, CHUNK)
    b = jnp.cumsum(logf.reshape(B, H, NC, CHUNK), axis=-1)
    bT = b[..., -1]
    a = bT[..., None] - b + li
    m_loc = jnp.max(a, axis=-1)
    wa = jnp.exp(a - m_loc[..., None])
    C_loc = jnp.einsum('bhnsd,bhnse->bhnde', kc * wa[..., None], vc)
    n_loc = jnp.einsum('bhns,bhnsd->bhnd', wa, kc)

    def step(carry, xs):
        C, n, m = carry
        Cl, nl, ml, bt = xs
        m_new = jnp.maximum(bt + m, ml)
        s_prev = jnp.exp(bt + m - m_new)
        s_loc = jnp.exp(ml - m_new)
        C_new = s_prev[..., None, None] * C + s_loc[..., None, None] * Cl
        n_new = s_prev[..., None] * n + s_loc[..., None] * nl
        return (C_new, n_new, m_new), (C, n, m)

    init = (jnp.zeros((B, H, DH, DH), f32), jnp.zeros((B, H, DH), f32), jnp.zeros((B, H), f32))
    xs = (jnp.moveaxis(C_loc, 2, 0), jnp.moveaxis(n_loc, 2, 0),
          jnp.moveaxis(m_loc, 2, 0), jnp.moveaxis(bT, 2, 0))
    _, (C_prev, n_prev, m_prev) = lax.scan(step, init, xs)
    C_prev = jnp.moveaxis(C_prev, 0, 2)
    n_prev = jnp.moveaxis(n_prev, 0, 2)
    m_prev = jnp.moveaxis(m_prev, 0, 2)

    mask = np.tril(np.ones((CHUNK, CHUNK), dtype=bool))
    Dlog = b[..., :, None] - b[..., None, :] + li[..., None, :]
    Dlog = jnp.where(mask, Dlog, -jnp.inf)
    inter = b + m_prev[..., None]
    m_t = jnp.maximum(inter, jnp.max(Dlog, axis=-1))
    w_inter = jnp.exp(inter - m_t)
    scores = jnp.einsum('bhntd,bhnsd->bhnts', qc, kc) * jnp.exp(Dlog - m_t[..., None])
    num = (w_inter[..., None] * jnp.einsum('bhntd,bhnde->bhnte', qc, C_prev)
           + jnp.einsum('bhnts,bhnse->bhnte', scores, vc))
    den = w_inter * jnp.einsum('bhntd,bhnd->bhnt', qc, n_prev) + jnp.sum(scores, axis=-1)
    h = num / jnp.maximum(jnp.abs(den), jnp.exp(-m_t))[..., None]
    return h.reshape(B, H, Lp, DH)

def mlstm_mixer(q, k, v, o, gates, gate_b, mh_g):
    B, L, _ = q.shape
    pad = (-L) % CHUNK
    Lp = L + pad

    def heads(t):
        t = jnp.pad(t, ((0, 0), (pad, 0), (0, 0)))
        return t.reshape(B, Lp, N_HEADS, HEAD_DIM).transpose(0, 2, 1, 3)

    g = gates.astype(jnp.float32).reshape(B, L, 4, N_HEADS) + gate_b.astype(jnp.float32)
    g = jnp.transpose(g, (2, 0, 3, 1))
    logi = jnp.pad(g[:2], ((0, 0), (0, 0), (0, 0), (pad, 0)), constant_values=NEG)
    logf = jnp.pad(jax.nn.log_sigmoid(g[2:]), ((0, 0), (0, 0), (0, 0), (pad, 0)), constant_values=0.0)
    qh, kh, vh = heads(q), heads(k), heads(v)
    h_f = mlstm_chunkwise(qh, kh, vh, logi[0], logf[0])
    h_b = jnp.flip(mlstm_chunkwise(jnp.flip(qh, 2), jnp.flip(kh, 2), jnp.flip(vh, 2),
                                   jnp.flip(logi[1], -1), jnp.flip(logf[1], -1)), 2)
    h = (h_f + h_b)[:, :, pad:]
    h = h * lax.rsqrt(jnp.mean(h * h, axis=-1, keepdims=True) + EPS)
    h = h.transpose(0, 2, 1, 3).reshape(B, L, D_MLSTM) * mh_g.astype(jnp.float32)
    return (h * jax.nn.sigmoid(o.astype(jnp.float32))).astype(q.dtype)

def centred_dwconv(x, w, b):
    C = x.shape[-1]
    y = lax.conv_general_dilated(x, w[:, None, :], window_strides=(1,), padding='SAME',
                                 dimension_numbers=('NWC', 'WIO', 'NWC'), feature_group_count=C)
    return y + b

def expert_choice_ffn(h, w_router, w_gate, w_up, w_down):
    B, L, D = h.shape
    N = B * L
    t = h.reshape(N, D)
    cap = CAPACITY_FACTOR * N // N_EXPERTS
    aff = jax.nn.softmax(jnp.matmul(t, w_router).astype(jnp.float32), axis=-1)
    gate, idx = lax.top_k(aff.T, cap)
    xe = t[idx]
    hid = jax.nn.silu(jnp.einsum('ecd,edf->ecf', xe, w_gate)) * jnp.einsum('ecd,edf->ecf', xe, w_up)
    ye = jnp.einsum('ecf,efd->ecd', hid, w_down) * gate[..., None].astype(hid.dtype)
    out = jnp.zeros((N, D), ye.dtype).at[idx.reshape(-1)].add(ye.reshape(-1, D))
    return out.reshape(B, L, D).astype(h.dtype)

def trunk(x, meta_tokens, norm1_g, w_in, conv_w, conv_b, gate_b, pool_w, pool_scale,
          mh_norm_g, w_out, norm2_g, w_router, w_gate, w_up, w_down, final_g):
    B = x.shape[0]
    meta = jnp.broadcast_to(meta_tokens[None].astype(x.dtype), (B, N_META, D_MODEL))
    x = jnp.concatenate([meta, x], axis=1)
    o1 = D_POOL
    o2 = o1 + D_MLSTM
    o3 = o2 + D_MLSTM
    o4 = o3 + D_MLSTM
    o5 = o4 + D_MLSTM
    for l in range(DEPTH):
        h = rmsnorm(x, norm1_g[l])
        z = jnp.matmul(h, w_in[l])
        u = z[..., :o1]
        qk = jax.nn.silu(centred_dwconv(z[..., o1:o3], conv_w[l], conv_b[l]))
        q, k = qk[..., :D_MLSTM], qk[..., D_MLSTM:]
        v, o, gates = z[..., o3:o4], z[..., o4:o5], z[..., o5:]
        y_pool = pool_mixer(u, pool_w[l], pool_scale[l]).astype(x.dtype)
        y_mlstm = mlstm_mixer(q, k, v, o, gates, gate_b[l], mh_norm_g[l]).astype(x.dtype)
        x = x + jnp.matmul(jnp.concatenate([y_pool, y_mlstm], axis=-1), w_out[l])
        x = x + expert_choice_ffn(rmsnorm(x, norm2_g[l]), w_router[l], w_gate[l], w_up[l], w_down[l])
    return rmsnorm(x, final_g)[:, N_META:]

def setup_inputs(seed: int = 0) -> dict:
    key = jax.random.key(seed)
    ks = jax.random.split(key, 20)
    f32 = jnp.float32
    nrm = lambda k, s, sc: jax.random.normal(k, s, f32) * sc
    gate_base = jnp.array([0.0, 0.0, 3.0, 3.0], f32)[None, :, None]
    return {
        "x_prompt": nrm(ks[0], (BATCH, SEQ, D_MODEL), 1.0),
        "x_sample": nrm(ks[1], (DEC_BATCH, DEC_SEQ, D_MODEL), 1.0),
        "meta_tokens": nrm(ks[2], (N_META, D_MODEL), 1.0),
        "norm1_g": 1.0 + nrm(ks[3], (DEPTH, D_MODEL), 0.02),
        "w_in": nrm(ks[4], (DEPTH, D_MODEL, N_IN), D_MODEL ** -0.5),
        "conv_w": nrm(ks[5], (DEPTH, CONV_K, 2 * D_MLSTM), CONV_K ** -0.5),
        "conv_b": nrm(ks[6], (DEPTH, 2 * D_MLSTM), 0.01),
        "gate_b": gate_base + nrm(ks[7], (DEPTH, 4, N_HEADS), 0.3),
        "pool_w": nrm(ks[8], (DEPTH, N_POOL_GROUPS, D_POOL_GROUP, D_POOL_GROUP), D_POOL_GROUP ** -0.5),
        "pool_scale": 1.0 + nrm(ks[9], (DEPTH, D_POOL), 0.02),
        "mh_norm_g": 1.0 + nrm(ks[10], (DEPTH, D_MLSTM), 0.02),
        "w_out": nrm(ks[11], (DEPTH, D_MIX, D_MODEL), D_MIX ** -0.5),
        "norm2_g": 1.0 + nrm(ks[12], (DEPTH, D_MODEL), 0.02),
        "w_router": nrm(ks[13], (DEPTH, D_MODEL, N_EXPERTS), D_MODEL ** -0.5),
        "w_gate": nrm(ks[14], (DEPTH, N_EXPERTS, D_MODEL, D_FF), D_MODEL ** -0.5),
        "w_up": nrm(ks[15], (DEPTH, N_EXPERTS, D_MODEL, D_FF), D_MODEL ** -0.5),
        "w_down": nrm(ks[16], (DEPTH, N_EXPERTS, D_FF, D_MODEL), D_FF ** -0.5),
        "final_g": 1.0 + nrm(ks[17], (D_MODEL,), 0.02),
    }

def reference(x_prompt, x_sample, meta_tokens, norm1_g, w_in, conv_w, conv_b, gate_b, pool_w,
              pool_scale, mh_norm_g, w_out, norm2_g, w_router, w_gate, w_up, w_down, final_g):
    y_prompt = trunk(x_prompt, meta_tokens, norm1_g, w_in, conv_w, conv_b, gate_b, pool_w, pool_scale,
                     mh_norm_g, w_out, norm2_g, w_router, w_gate, w_up, w_down, final_g)
    y_sample = trunk(x_sample, meta_tokens, norm1_g, w_in, conv_w, conv_b, gate_b, pool_w, pool_scale,
                     mh_norm_g, w_out, norm2_g, w_router, w_gate, w_up, w_down, final_g)
    return (y_prompt, y_sample)


_drawn_inputs = setup_inputs


def setup_inputs(seed=0):
    import zlib

    import numpy as np

    out = dict(_drawn_inputs(seed))
    spreads = {}
    factors = {'norm1_g': 3.059,
     'conv_b': 37.131,
     'pool_scale': 4.212,
     'mh_norm_g': 11.78,
     'norm2_g': 3.659,
     'final_g': 8.214}
    for name, (base, spread) in spreads.items():
        noise = np.random.default_rng([zlib.crc32(name.encode()), seed]).standard_normal(out[name].shape)
        drawn = base * np.exp(spread * noise) if base else spread * noise
        out[name] = __import__('jax').numpy.asarray(drawn.astype(out[name].dtype))
    for name, factor in factors.items():
        out[name] = (out[name] * factor).astype(out[name].dtype)
    return out
```

```python
import math

import numpy as np
import concourse.bass as bass
from concourse import mybir
from concourse.alu_op_type import AluOpType as ALU
from contextlib import ExitStack

F32 = mybir.dt.float32
BF16 = mybir.dt.bfloat16
U32 = mybir.dt.uint32
ACT = mybir.ActivationFunctionType
AX = mybir.AxisListType

P = 128
D = 1024
KT = D // P
N_META, PAD = 16, 48
SEQ_P, SEQ_S = 256, 1024
BOUND = PAD + N_META + SEQ_P
T = BOUND + PAD + N_META + SEQ_S
NT = T // P
BT = BOUND // P
REAL = ((PAD, BOUND), (BOUND + PAD, T))
D_POOL, D_ML = 256, 768
HD = 192
PAIR = 2 * HD
VW = HD + 1
NE = 16
CAP_P, CAP_S = 2 * 272 // NE, 2 * 1040 // NE
SLOTS = CAP_P + CAP_S
SB_ROWS = SLOTS - P
EPS = 1e-6
NEG = -1e30
LN_SCALE = math.log(HD ** -0.5)
CHUNKS = ((0, 512), (512, 1024), (1024, T))
BW = 32
NR = BW + 4


def layout():
    o, at = {}, 0
    for name, n in (("hT", KT * T), ("qT", 3 * T), ("kT", 3 * T), ("og", NT * PAIR), ("v", NT * 2 * VW + 2),
                    ("Cb", NT * 3 * VW + 1), ("W", 2 * KT * PAIR), ("Z", 1424), ("negM", T), ("E", 512),
                    ("Pm", 512), ("inter", 4 * VW), ("num", 4 * VW), ("kw", 2 * PAIR), ("Cf", 3 * VW + 1),
                    ("hh", 2 * PAIR), ("mhg", PAIR), ("q1h", T), ("pw", 2 * P), ("junk", HD)):
        o[name] = at
        at += n
    o["end"] = at
    return o


def bank_plan():
    keys = []
    for i in range(NT):
        keys += [("x", i, 0), ("x", i, 1)]
    keys += [("par",)]
    for i in range(NT + 1):
        if i < NT:
            keys.append(("g", i))
        if i:
            keys.append(("gt", i - 1))
    keys += [("u", j, c) for j in range(2) for c in range(3)]
    for p in range(2):
        keys += [("qk", p, 0, j, c) for j in range(3) for c in range(3)]
        if p == 0:
            keys += [("po", j, g) for j in range(2) for g in range(3)]
        keys += [("qk", p, 1, j, c) for j in range(3) for c in range(3)]
        if p == 0:
            keys += [("rc", i) for i in range(NT)] + [("sp",)]
        keys += [("vo", p, i, w) for w in range(2) for i in range(NT)]
        for i in range(NT - 1, 0, -1):
            keys += [("kb", p, i), ("cb0", p, i), ("cb1", p, i)]
        for i in range(NT):
            keys += [("S", p, i), ("kf", p, i), ("cf0", p, i), ("cf1", p, i)]
    for i in range(NT + 1):
        if i == 0:
            keys += [("yT", 0, 0), ("yT", 0, 1)]
        if i < NT:
            keys += [("wo", i, 0), ("wo", i, 1)]
            if i + 1 < NT:
                keys += [("yT", i + 1, 0), ("yT", i + 1, 1)]
        if i:
            keys += [("tT", i - 1, 0), ("tT", i - 1, 1), ("lg", i - 1)]
    keys += [("af", g) for g in range(3)] + [("ix",)]
    plan, used = {}, [0, 0, 0]
    for n, key in enumerate(keys):
        used[n % 3] += 1
        plan[key] = (n % 3, used[n % 3])
    return plan


class Steps:

    def __init__(self, eng, sem):
        self.eng, self.sem, self.n = eng, sem, 0

    def do(self, ins):
        ins.then_inc(self.sem, 1)
        self.n += 1
        return self.n

    def settle(self):
        self.eng.wait_ge(self.sem, self.n)


def encoder_program(nc, x_prompt, x_sample, meta, g1, w_in, conv_w, conv_b, gate_b, pool_w, pool_scale,
                    mh_g, w_out, g2, w_router, w_gate, w_up, w_down, final_g, rcount, y_prompt, y_sample):
    plan, off = bank_plan(), layout()
    y_d = nc.dram_tensor("mixer_out", (T, D), F32, kind="Internal").ap()
    t_d = nc.dram_tensor("ffn_in", (T, D), F32, kind="Internal").ap()
    acc_d = nc.dram_tensor("residual", (T, D), F32, kind="Internal").ap()

    ctx = ExitStack()
    with ctx:
        def sb(name, shape, dt=F32):
            return ctx.enter_context(nc.sbuf_tensor(name, shape, dt))

        def sem(name):
            return ctx.enter_context(nc.semaphore(name))

        arena = sb("arena", [P, off["end"]])

        def area(name, n, parts=P, shift=0):
            a = off[name] + shift if isinstance(name, str) else name + shift
            return arena[0:parts, a:a + n]

        ident = sb("ident", [P, P])
        ident_b = sb("ident_b", [P, P], BF16)
        masks = sb("masks", [P, 2, 2, P], BF16)
        cols = sb("cols", [P, NT, 4, NR])
        spc = sb("spc", [P, 12, NT])
        par = sb("par", [P, 56])
        small = sb("small", [P, 96])
        ss_h = sb("ss_h", [P, 2 * NT])
        gb = sb("gb", [NR, 2])
        S0 = sb("S0", [NR, NT])
        S1 = sb("S1", [NR, NT])
        ps = [ctx.enter_context(nc.psum_tensor(f"bank{b}", [P, 512], F32)) for b in range(8)]

        hT = area("hT", KT * T).rearrange("p (k t) -> p k t", k=KT)
        qT = area("qT", 3 * T).rearrange("p (j t) -> p j t", j=3)
        kT = area("kT", 3 * T).rearrange("p (j t) -> p j t", j=3)
        qkT = (qT, kT)
        q1h = area("q1h", T)
        og = area("og", NT * PAIR).rearrange("p (i h d) -> p i h d", i=NT, h=2)
        v = area("v", NT * 2 * VW).rearrange("p (i h d) -> p i h d", i=NT, h=2)
        Cb = area("Cb", NT * 3 * VW).rearrange("p (i j d) -> p i j d", i=NT, j=3)
        Cf = area("Cf", 3 * VW).rearrange("p (j d) -> p j d", j=3)
        Wb = [area("W", KT * PAIR, shift=s * KT * PAIR).rearrange("p (k n) -> p k n", k=KT) for s in range(2)]
        Z = area("Z", 1424)
        negM = area("negM", T, NR)
        E = area("E", 512)
        Pm = area("Pm", 512)
        inter = area("inter", 4 * VW).rearrange("p (q d) -> p q d", q=4)
        num = area("num", 4 * VW).rearrange("p (q d) -> p q d", q=4)
        kw = area("kw", 2 * PAIR).rearrange("p (s h d) -> p s h d", s=2, h=2)
        hh = area("hh", 2 * PAIR).rearrange("p (s h d) -> p s h d", s=2, h=2)
        mhg = area("mhg", PAIR)
        Wg = area("kw", KT * 2 * NR).rearrange("p (k n) -> p k n", k=KT)
        pw = area("pw", 2 * P).rearrange("p (j n) -> p j n", j=2)
        psc = area("num", 2 * P).rearrange("p (j n) -> p j n", j=2)
        xin = [area("qT", D, shift=s * D) for s in range(2)]
        xn = [area("qT", D, shift=(2 + s) * D) for s in range(2)]
        g1b = area("kT", D)
        gtok = area("Z", NT * 2 * NR).rearrange("p (i n) -> p i n", i=NT)
        prow = area("E", P, 48)
        R = [area("v", T, NR, shift=n * T) for n in range(7)]
        R01 = area("v", 2 * T, NR).rearrange("p (r t) -> p r t", r=2)
        U, PA, PB = (area("kT", 1424, shift=n * 1424) for n in range(3))
        rc_t = area("kT", T, shift=3 * 1424)
        mix0 = area("kT", T, shift=3 * 1424 + T)
        ypool = area("hh", 512)
        junk_h = area("junk", HD)
        wout = area(0, KT * D).rearrange("p (k n) -> p k n", k=KT)
        wout_in = sem("wout_in")
        junk_b = area(47 * D, D)

        full = [sem(f"bank{b}_full") for b in range(8)]
        free = [sem(f"bank{b}_free") for b in range(8)]
        x_in = [sem("x_in0"), sem("x_in1")]
        x_clear = sem("x_clear")
        sq_done = sem("sq_done")
        xn_done = sem("xn_done")
        params_in = sem("params_in")
        prow_in, gw_in, gb_in = sem("prow_in"), sem("gw_in"), sem("gb_in")
        pool_par_in, mhg_in = sem("pool_par_in"), sem("mhg_in")
        zeroed = sem("zeroed")
        ident_done = sem("ident_done")
        masks_done = sem("masks_done")
        w_slot_in = [sem("w_slot0_in"), sem("w_slot1_in")]
        act_step, dve_step, pool_step = sem("act_step"), sem("dve_step"), sem("pool_step")
        rows_dve = sem("rows_dve")
        rows_act = sem("rows_act")
        rows_ready = sem("rows_ready")
        mixed_ready = sem("mixed_ready")
        pw_ready = sem("pw_ready")
        ypool_out = sem("ypool_out")
        centre_tap = sem("centre_tap")
        taps_done = sem("taps_done")
        silu_done = sem("silu_done")
        og_ready = sem("og_ready")
        ones_set = sem("ones_set")
        hh_ready, hh_sq = sem("hh_ready"), sem("hh_sq")
        y_raw = sem("y_raw")
        ms_ready, rms_ready, rs_ready = sem("ms_ready"), sem("rms_ready"), sem("rs_ready")
        y_scaled, y_out = sem("y_scaled"), sem("y_out")

        x_rows = {0: [(PAD, meta[:, :]), (64, x_prompt[0, 0:64, :])],
                  1: [(0, x_prompt[0, 64:192, :])],
                  2: [(0, x_prompt[0, 192:256, :]), (112, meta[:, :])]}
        for i in range(3, NT):
            x_rows[i] = [(0, x_sample[0, (i - 3) * P:(i - 2) * P, :])]

        def x_count(i):
            return 16 * sum(len(x_rows[n]) for n in range(i % 2, i + 1, 2))

        w_blocks = [(0, D_POOL)] + [(D_POOL + w * D_ML + p * PAIR, PAIR) for p in range(2) for w in range(4)]

        def tile_cols(i):
            return slice(i * P, (i + 1) * P)

        def row(direction, head):
            return direction * BW + head

        def multiplied(eng, key):
            b, k = plan[key]
            eng.wait_ge(full[b], k)

        def read_out(eng, key):
            b, k = plan[key]
            eng.wait_ge(free[b], k)

        state_key = [k for p in range(2) for k in
                     [("cb1", p, i) for i in range(NT - 1, 0, -1)] + [("cf1", p, i) for i in range(NT)]]
        kw_key = [k for p in range(2) for k in
                  [("kb", p, i) for i in range(NT - 1, 0, -1)] + [("kf", p, i) for i in range(NT)]]
        block_last = [("u", 1, 2)] + [k for p in range(2) for k in
                                      (("qk", p, 0, 2, 2), ("qk", p, 1, 2, 2), ("vo", p, NT - 1, 0), ("vo", p, NT - 1, 1))]

        ORDER = [(1, 0), (1, 1), (0, 0), (0, 1)]


        with nc.Block() as block:
            @block.sync
            def _(sp):
                w_view = w_in[0].rearrange("(k p) n -> p k n", p=P)

                def load_w(n):
                    c, w = w_blocks[n]
                    if n >= 2:
                        multiplied(sp, block_last[n - 2])
                    sp.dma_start(Wb[n % 2][:, :, 0:w], w_view[:, :, c:c + w]).then_inc(w_slot_in[n % 2], 16)

                def load_x(i):
                    if i in (0, BT):
                        sp.wait_ge(x_clear, 1 if i == 0 else 2)
                    if i >= 2:
                        sp.wait_ge(xn_done, i - 1)
                        sp.wait_ge(sq_done, i - 1)
                    for p0, src in x_rows[i]:
                        sp.dma_start(xin[i % 2][p0:p0 + src.shape[0], :], src).then_inc(x_in[i % 2], 16)

                load_x(1)
                load_x(0)
                sp.dma_start(g1b, g1[0:1, :].to_broadcast([P, D])).then_inc(params_in, 16)
                sp.wait_ge(zeroed, 2)
                gw = w_in[0][:, 3328:3344].rearrange("(k p) n -> p k n", p=P)
                with nc.allow_non_contiguous_dma(reason="gate columns"):
                    for n, (what, d) in enumerate(((0, 0), (0, 1), (1, 0), (1, 1))):
                        src = gw[:, :, (2 * what + d) * 4:(2 * what + d) * 4 + 4]
                        c = what * NR + d * BW
                        sp.dma_start(Wg[:, :, c:c + 4], src).then_inc(gw_in, 16)
                        sp.dma_start(gb[d * BW:d * BW + 4, what:what + 1],
                                     gate_b[0, 2 * what + d:2 * what + d + 1, :].rearrange("a h -> h a")).then_inc(gb_in, 16)
                sp.dma_start(prow[0:36, :], conv_w[0].rearrange("k (c p) -> (k c) p", p=P)).then_inc(prow_in, 16)
                sp.dma_start(prow[36:48, :], conv_b[0].rearrange("(c p) -> c p", p=P)).then_inc(prow_in, 16)
                load_w(0)
                for i in range(2, NT):
                    load_x(i)
                load_w(1)
                for j in range(2):
                    for g in range(2):
                        sp.dma_start(pw[64 * g:64 * g + 64, j, 64 * g:64 * g + 64], pool_w[0, 2 * j + g, :, :]).then_inc(pool_par_in, 16)
                    sp.dma_start(psc[:, j, :], pool_scale[0:1, j * P:(j + 1) * P].to_broadcast([P, P])).then_inc(pool_par_in, 16)
                sp.dma_start(mhg, mh_g[0:1, 0:PAIR].to_broadcast([P, PAIR])).then_inc(mhg_in, 16)
                for j in range(2):
                    if j:
                        sp.wait_ge(mixed_ready, 1)
                    for g in range(2):
                        sp.dma_start(rc_t[64 * g:64 * g + 64, :], rcount[2 * j + g:2 * j + g + 1, :].to_broadcast([64, T])).then_inc(params_in, 16)
                for n in range(2, len(w_blocks)):
                    load_w(n)
                    if n == 3:
                        for j in range(2):
                            for g in range(3):
                                read_out(sp, ("po", j, g))
                                lo, hi = 4 * g, min(4 * g + 4, NT)
                                sp.dma_start(y_d[lo * P:hi * P, j * P:(j + 1) * P].rearrange("(i p) n -> p i n", p=P),
                                             ypool[:, 0:(hi - lo) * P].rearrange("p (i n) -> p i n", n=P)).then_inc(ypool_out, 16)
                    if n == 6:
                        sp.wait_ge(og_ready, NT)
                        sp.dma_start(mhg, mh_g[0:1, PAIR:D_ML].to_broadcast([P, PAIR])).then_inc(mhg_in, 16)
                        sp.wait_ge(y_scaled, 1)
                        sp.dma_start(y_d[:, D_POOL:D_POOL + PAIR].rearrange("(i p) n -> p i n", p=P),
                                     area("og", NT * PAIR).rearrange("p (i n) -> p i n", i=NT)).then_inc(y_out, 16)
                multiplied(sp, ("vo", 1, NT - 1, 1))
                sp.dma_start(wout, w_out[0].rearrange("(k p) n -> p k n", p=P)).then_inc(wout_in, 16)
                sp.wait_ge(y_scaled, 2)
                sp.dma_start(y_d[:, D_POOL + PAIR:D].rearrange("(i p) n -> p i n", p=P),
                             area("og", NT * PAIR).rearrange("p (i n) -> p i n", i=NT)).then_inc(y_out, 16)
                sp.wait_ge(y_out, 32)
                sp.wait_ge(ypool_out, 96)

            @block.gpsimd
            def _(pool):
                st = Steps(pool, pool_step)
                st.do(pool.memset(ident[:, :], 0.0))
                st.do(pool.memset(masks[:, :, :, :], 0.0))
                st.settle()
                pool.affine_select(out=ident[:, :], in_=ident[:, :], compare_op=ALU.not_equal, fill=1.0, base=0,
                                   pattern=[[-1, P]], channel_multiplier=1).then_inc(ident_done, 1)
                for b in range(2):
                    for q, d in enumerate((1, 0)):
                        sgn = 1 if d == 0 else -1
                        st.do(pool.affine_select(out=masks[:, b, q, :], in_=masks[:, b, q, :], compare_op=ALU.is_ge,
                                                 fill=NEG, base=0, pattern=[[sgn, P]], channel_multiplier=-sgn))
                st.settle()
                half = BOUND % P
                st.do(pool.memset(masks[0:half, 1, :, half:P], NEG))
                st.settle()
                pool.memset(masks[half:P, 1, :, 0:half], NEG).then_inc(masks_done, 1)

                pool.wait_ge(masks_done, 1)
                pool.wait_ge(pool_par_in, 96)
                pool.tensor_tensor(pw[:, :, :], pw[:, :, :], psc[:, :, :], ALU.mult).then_inc(pw_ready, 1)

                def shifted(out, a, lo, hi, d0, d1, parts=slice(0, P)):
                    st.do(pool.tensor_tensor(out[parts, lo:hi], a[parts, lo + d0:hi + d0], a[parts, lo + d1:hi + d1], ALU.add))
                    st.settle()

                lo_h, hi_h = slice(0, 64), slice(64, P)
                body = slice(8, 8 + T)
                for j in range(2):
                    read_out(pool, ("u", j, 2))
                    shifted(PA, U, 1, 1424, -1, 0)
                    shifted(PB, PA, 2, 1423, -1, 1)
                    dst = mix0 if j == 0 else PA[:, body]
                    if j == 1:
                        shifted(PA, PB, 4, 1421, -2, 2)
                        shifted(PB, PA, 8, 1416, -4, 4, hi_h)
                    pool.wait_ge(params_in, 16 + 32 * (j + 1))
                    st.do(pool.tensor_tensor(dst[lo_h, :], PA[lo_h, body], rc_t[lo_h, :], ALU.mult))
                    st.settle()
                    st.do(pool.tensor_tensor(dst[hi_h, :], PB[hi_h, body], rc_t[hi_h, :], ALU.mult))
                    st.settle()
                    pool.tensor_tensor(dst, dst, U[:, body], ALU.subtract).then_inc(mixed_ready, 1)

                for p in range(2):
                    for i in range(NT):
                        read_out(pool, ("vo", p, i, 1))
                        if i == 0:
                            pool.wait_ge(mhg_in, 16 * (p + 1))
                        pool.tensor_tensor(og[:, i, :, :], og[:, i, :, :],
                                           mhg.rearrange("p (h d) -> p h d", h=2), ALU.mult).then_inc(og_ready, 1)
                    for i in range(NT):
                        pool.wait_ge(hh_ready, p * NT + i + 1)
                        pool.wait_ge(og_ready, p * NT + i + 1)
                        pool.tensor_tensor(og[:, i, :, :], og[:, i, :, :], hh[:, i % 2, :, :], ALU.mult).then_inc(y_raw, 1)
                    pool.wait_ge(rs_ready, p + 1)
                    pool.wait_ge(y_raw, (p + 1) * NT)
                    ogf = area("og", NT * PAIR).rearrange("p (n d) -> p n d", d=HD)
                    pool.tensor_tensor(ogf, ogf, ss_h[:, :].unsqueeze(2).to_broadcast([P, 2 * NT, HD]), ALU.mult).then_inc(y_scaled, 1)

            @block.scalar
            def _(act):
                st = Steps(act, act_step)

                def evac(key, out, src, func=ACT.Copy, **kw_):
                    b, k = plan[key]
                    act.wait_ge(full[b], k)
                    return act.activation(out, src(ps[b]), func, **kw_).then_inc(free[b], 1)

                def move_xT(i):
                    for h in range(2):
                        evac(("x", i, h), hT[:, 4 * h:4 * h + 4, tile_cols(i)], lambda b: b[:, :].rearrange("p (k t) -> p k t", k=4))

                for i in range(NT):
                    act.wait_ge(x_in[i % 2], x_count(i))
                    st.do(act.activation(area("Pm", D), xin[i % 2], ACT.Square, accum_out=small[:, i:i + 1]))
                    st.settle()
                    st.do(act.activation(small[:, 16 + i:17 + i], small[:, i:i + 1], ACT.Copy, scale=1.0 / D, bias=EPS))
                    st.settle()
                    act.activation(small[:, 32 + i:33 + i], small[:, 16 + i:17 + i], ACT.Sqrt).then_inc(sq_done, 1)
                    if i:
                        move_xT(i - 1)
                move_xT(NT - 1)
                evac(("par",), par[:, 0:48], lambda b: b[:, 0:48])
                for i in range(NT):
                    evac(("g", i), gtok[:, i, :], lambda b: b[:, 0:2 * NR])
                act.wait_ge(rows_dve, 1)
                st.do(act.activation(R[2], R[1], ACT.Abs))
                st.settle()
                st.do(act.activation(R[2], R[2], ACT.Exp, scale=-1.0))
                st.settle()
                act.activation(R[2], R[2], ACT.Ln, bias=1.0).then_inc(rows_act, 1)
                for j in range(2):
                    if j:
                        act.wait_ge(mixed_ready, 1)
                    for c, (lo, hi) in enumerate(CHUNKS):
                        b, k = plan[("u", j, c)]
                        act.wait_ge(full[b], k)
                        if j == 0 and c == 0:
                            act.wait_ge(zeroed, 3)
                        act.activation(U[:, 8 + lo:8 + hi], ps[b][:, 0:hi - lo], ACT.Copy).then_inc(free[b], 1)

                def rows_out(out, src, func, **kw_):
                    st.do(act.activation(out[0:BW, :], src[0:BW, :], func, **kw_))
                    st.do(act.activation(out[BW:NR, :], src[BW:NR, ::-1], func, **kw_))

                def gate_rows():
                    act.wait_ge(rows_dve, 2)
                    for lo_p, hi_p, rev in ((0, BW, slice(None)), (BW, NR, slice(None, None, -1))):
                        st.do(act.activation(R[1][lo_p:hi_p, :], R[2][lo_p:hi_p, rev], ACT.Exp, bias=small[lo_p:hi_p, 95:96]))
                    rows_out(S1[:, :], S0[:, :], ACT.Exp)
                    st.settle()
                    rows_out(R[2], R[6], ACT.Exp)
                    rows_out(R[3], R[5], ACT.Exp, scale=-1.0)
                    rows_out(negM, R[4], ACT.Copy, scale=-1.0)
                    st.settle()
                    rows_out(R[5], R[0], ACT.Copy, bias=LN_SCALE)
                    st.settle()
                    act.sem_inc(rows_ready, 1)

                def conv_centre(p, w, j):
                    n = (p * 2 + w) * 3 + j
                    if n:
                        act.wait_ge(taps_done, n)
                    if n == 3:
                        b, k = plan[("po", 1, 2)]
                        act.wait_ge(full[b], k)
                    for c, (lo, hi) in enumerate(CHUNKS):
                        b, k = plan[("qk", p, w, j, c)]
                        act.wait_ge(full[b], k)
                        if n == 0 and c == 0:
                            act.wait_ge(zeroed, 4)
                        act.activation(Z[:, 1 + lo:1 + hi], ps[b][:, 0:hi - lo], ACT.Copy).then_inc(free[b], 1)
                    act.wait_ge(free[b], k)
                    ct = w * 6 + p * 3 + j
                    act.activation(qkT[w][:, j, :], Z[:, 1:1 + T], ACT.Identity, scale=par[:, 12 + ct:13 + ct],
                                   bias=par[:, 36 + ct:37 + ct]).then_inc(centre_tap, 1)

                def silu(p, w, j):
                    n = (p * 2 + w) * 3 + j
                    act.wait_ge(taps_done, n + 1)
                    if w == 0 and j == 1:
                        if p == 0:
                            act.wait_ge(zeroed, 5)
                        st.do(act.activation(q1h[64:P, :], qT[64:P, 1, :], ACT.Silu))
                        st.do(act.activation(qT[0:64, 1, :], qT[0:64, 1, :], ACT.Silu))
                        act.memzero(qT[64:P, 1, :]).then_inc(silu_done, 1)
                    else:
                        act.activation(qkT[w][:, j, :], qkT[w][:, j, :], ACT.Silu).then_inc(silu_done, 1)

                def weigh_keys(key, p, i, d, n):
                    b, k = plan[key]
                    act.wait_ge(full[b], k)
                    if n >= 2:
                        multiplied(act, state_key[n - 2])
                    for h in range(2):
                        r = row(d, 2 * p + h)
                        last = act.activation(kw[:, n % 2, h, :], ps[b][:, h * HD:(h + 1) * HD], ACT.Copy, scale=cols[:, i, 1, r:r + 1])
                    last.then_inc(free[b], 1)

                def decays(p, i, n):
                    act.wait_ge(full[3], n + 1)
                    if n:
                        read_out(act, ("S", (n - 1) // NT, (n - 1) % NT))
                    for q, (d, h) in enumerate(ORDER):
                        r = row(d, 2 * p + h)
                        last = act.activation(E[:, q * P:(q + 1) * P], ps[3][:, q * P:(q + 1) * P], ACT.Exp,
                                              bias=cols[:, i, 3, r:r + 1])
                    last.then_inc(free[3], 1)

                def square_hh(p, i):
                    act.wait_ge(hh_ready, p * NT + i + 1)
                    if p and i == 0:
                        act.wait_ge(y_scaled, 1)
                    for h in range(2):
                        act.wait_ge(hh_sq, 2 * (p * NT + i) + h) if p + i + h else None
                        act.activation(junk_h, hh[:, i % 2, h, :], ACT.Square, accum_out=ss_h[:, 2 * i + h:2 * i + h + 1]).then_inc(hh_sq, 1)

                for p in range(2):
                    for w in range(2):
                        for j in range(3):
                            conv_centre(p, w, j)
                            silu(p, w, j)
                            if p == 0 and w == 0 and j == 0:
                                gate_rows()
                        if p == 0 and w == 0:
                            for n in range(6):
                                b, k = plan[("po", n // 3, n % 3)]
                                act.wait_ge(full[b], k)
                                if n:
                                    act.wait_ge(ypool_out, 16 * n)
                                wd = 512 if n % 3 < 2 else (NT - 8) * P
                                act.activation(ypool[:, 0:wd], ps[b][:, 0:wd], ACT.Copy).then_inc(free[b], 1)
                    if p == 0:
                        for i in range(NT):
                            evac(("rc", i), cols[:, i, :, :], lambda b: b[:, 0:4 * NR].rearrange("p (a n) -> p a n", a=4))
                        evac(("sp",), spc[:, :, :], lambda b: b[:, 0:12 * NT].rearrange("p (a n) -> p a n", a=12))
                        b, k = plan[("sp",)]
                        act.wait_ge(free[b], k)
                    for i in range(NT):
                        b, k = plan[("vo", p, i, 0)]
                        if i == 0:
                            act.wait_ge(ones_set, 1)
                        evac(("vo", p, i, 0), v[:, i, :, 0:HD], lambda b: b[:, 0:PAIR].rearrange("p (h d) -> p h d", h=2))
                    if p == 1:
                        act.wait_ge(y_out, 16)
                    for i in range(NT):
                        evac(("vo", p, i, 1), og[:, i, :, :], lambda b: b[:, 0:PAIR].rearrange("p (h d) -> p h d", h=2), ACT.Sigmoid)
                    n = p * (2 * NT - 1)
                    for i in range(NT - 1, 0, -1):
                        weigh_keys(("kb", p, i), p, i, 1, n)
                        n += 1
                    decays(p, 0, p * NT)
                    for i in range(NT):
                        weigh_keys(("kf", p, i), p, i, 0, n)
                        n += 1
                        m = p * NT + i
                        for half in range(2):
                            act.wait_ge(full[4 + half], m + 1)
                            if m and half == 0:
                                act.wait_ge(free[7], m)
                            for hd in range(2):
                                q = 2 * half + hd
                                r = row(ORDER[q][0], 2 * p + hd)
                                last = act.activation(inter[:, q, :], ps[4 + half][:, hd * VW:(hd + 1) * VW], ACT.Copy,
                                                      scale=cols[:, i, 0, r:r + 1])
                            last.then_inc(free[4 + half], 1)
                        if i + 1 < NT:
                            decays(p, i + 1, m + 1)
                        if i:
                            square_hh(p, i - 1)
                    square_hh(p, NT - 1)
                    act.wait_ge(ms_ready, p + 1)
                    act.activation(ss_h[:, :], ss_h[:, :], ACT.Sqrt).then_inc(rms_ready, 1)

            @block.vector
            def _(dve):
                st = Steps(dve, dve_step)
                dve.memset(xin[0][0:64, :], 0.0).then_inc(x_clear, 1)
                dve.memset(Wg[:, :, :], 0.0).then_inc(zeroed, 1)
                dve.memset(gb[:, :], 0.0).then_inc(zeroed, 1)
                st.do(dve.memset(q1h[0:64, :], 0.0))
                st.do(dve.memset(pw[:, :, :], 0.0))
                st.do(dve.memset(small[:, 95:96], LN_SCALE))
                dve.wait_ge(ident_done, 1)
                st.do(dve.tensor_copy(ident_b[:, :], ident[:, :]))
                for i in range(NT):
                    if i == BT:
                        dve.wait_ge(xn_done, 1)
                        dve.wait_ge(sq_done, 1)
                        dve.memset(xin[0][64:P, :], 0.0).then_inc(x_clear, 1)
                    dve.wait_ge(sq_done, i + 1)
                    st.do(dve.reciprocal(small[:, 48 + i:49 + i], small[:, 32 + i:33 + i]))
                    if i == 0:
                        dve.wait_ge(params_in, 16)
                    if i >= 2:
                        b, k = plan[("x", i - 2, 1)]
                        dve.wait_ge(full[b], k)
                    st.settle()
                    dve.scalar_tensor_tensor(xn[i % 2], xin[i % 2], small[:, 48 + i:49 + i], g1b, ALU.mult, ALU.mult).then_inc(xn_done, 1)
                st.do(dve.memset(R[6], 1.0))
                st.settle()
                st.do(dve.memset(R[6][:, 0:T:P], 0.0))
                st.do(dve.memset(R[6][0:4, BOUND:BOUND + 1], 0.0))
                st.do(dve.memset(R[6][BW:NR, T - BOUND:T - BOUND + 1], 0.0))
                for i in range(NT):
                    b, k = plan[("gt", i)]
                    dve.wait_ge(full[b], k)
                    src = ps[b][0:NR, 0:2 * P].rearrange("p (r t) -> p r t", r=2)
                    st.do(dve.tensor_copy(R01[0:BW, :, tile_cols(i)], src[0:BW, :, :]))
                    dve.tensor_copy(R01[BW:NR, :, tile_cols(NT - 1 - i)], src[BW:NR, :, ::-1]).then_inc(free[b], 1)
                dve.wait_ge(free[b], k)
                dve.memset(U[:, 0:8], 0.0)
                dve.memset(U[:, 8 + T:1424], 0.0).then_inc(zeroed, 1)
                dve.memset(Z[:, 0:1], 0.0)
                dve.memset(Z[:, 1 + T:2 + T], 0.0).then_inc(zeroed, 1)
                dve.sem_inc(zeroed, 1)
                dve.wait_ge(gb_in, 64)
                st.do(dve.tensor_scalar(R[0], R[0], gb[:, 0:1], None, ALU.add))
                st.do(dve.tensor_scalar(R[1], R[1], gb[:, 1:2], None, ALU.add))
                st.settle()
                dve.sem_inc(rows_dve, 1)
                dve.wait_ge(rows_act, 1)
                st.do(dve.scalar_tensor_tensor(R[1], R[1], 0.0, R[2], ALU.min, ALU.subtract))
                st.settle()
                for lo, _ in REAL:
                    for ap, c0 in ((slice(0, 4), lo - PAD), (slice(BW, NR), T - lo)):
                        st.do(dve.memset(R[0][ap, c0:c0 + PAD], NEG))
                        st.do(dve.memset(R[1][ap, c0:c0 + PAD], 0.0))
                st.settle()
                st.do(dve.tensor_tensor_scan(R[3], R[6], R[1], 0.0, ALU.mult, ALU.add))
                st.settle()
                st.do(dve.tensor_tensor(R[0], R[0], R[3], ALU.subtract))
                st.do(dve.memset(R[6], 0.0))
                st.settle()
                st.do(dve.tensor_copy(R[2], R[0]))
                st.do(dve.tensor_copy(R[6][:, P:T:P], R[3][:, P - 1:T - P:P]))
                st.settle()
                for ap, c0 in ((slice(0, 4), BOUND), (slice(BW, NR), T - BOUND)):
                    st.do(dve.memset(R[6][ap, c0:c0 + 1], NEG))
                    st.do(dve.tensor_scalar(R[2][ap, c0:c0 + 1], R[0][ap, c0:c0 + 1], 0.0, None, ALU.max))
                st.settle()
                st.do(dve.tensor_tensor_scan(R[4], R[6], R[2], 0.0, ALU.add, ALU.max))
                st.settle()
                st.do(dve.tensor_tensor(R[5], R[3], R[4], ALU.add))
                st.do(dve.memset(R[6][:, 0:P], 0.0))
                st.settle()

                def tiles(ap):
                    return ap.rearrange("p (i t) -> p i t", t=P)

                st.do(dve.tensor_copy(tiles(R[6])[:, 1:NT, :], R[5][:, P - 1:T - P:P].unsqueeze(2).to_broadcast([NR, NT - 1, P])))
                st.settle()
                st.do(dve.tensor_tensor(R[2], R[6], R[4], ALU.subtract))
                st.do(dve.tensor_tensor(S0[:, :], R[6][:, 0:T:P], R[4][:, P - 1:T:P], ALU.subtract))
                st.settle()
                half = BOUND % P
                for ap, c0, s in ((slice(0, 4), BOUND, BT), (slice(BW, NR), T - BOUND, NT - 1 - BT)):
                    st.do(dve.memset(R[2][ap, c0:c0 + P - half], NEG))
                    st.do(dve.memset(S0[ap, s:s + 1], NEG))
                st.do(dve.tensor_tensor(tiles(R[6]), tiles(R[0]), R[4][:, P - 1:T:P].unsqueeze(2).to_broadcast([NR, NT, P]), ALU.subtract))
                st.settle()
                for ap, c0 in ((slice(0, 4), BOUND), (slice(BW, NR), T - BOUND)):
                    st.do(dve.memset(R[6][ap, c0 - half:c0], NEG))
                st.settle()
                dve.sem_inc(rows_dve, 1)

                def outer_taps(p, w, j):
                    n = (p * 2 + w) * 3 + j
                    ct = w * 6 + p * 3 + j
                    dve.wait_ge(centre_tap, n + 1)
                    o = qkT[w][:, j, :]
                    st.do(dve.scalar_tensor_tensor(o, Z[:, 0:T], par[:, ct:ct + 1], o, ALU.mult, ALU.add))
                    st.settle()
                    dve.scalar_tensor_tensor(o, Z[:, 2:2 + T], par[:, 24 + ct:25 + ct], o, ALU.mult, ALU.add).then_inc(taps_done, 1)

                def update_state(new, old, k0, k1, p, d, i):
                    for j in range(3):
                        b, k = plan[k0 if j < 2 else k1]
                        if j != 1:
                            dve.wait_ge(full[b], k)
                        a = (p * 2 + d) * 3 + j
                        c = (j % 2) * VW
                        last = dve.scalar_tensor_tensor(new[:, j, :], old[:, j, :], spc[:, a, i:i + 1], ps[b][:, c:c + VW], ALU.mult, ALU.add)
                        if j == 0:
                            st.do(last)
                        else:
                            last.then_inc(free[b], 1)
                    dve.wait_ge(free[b], k)

                for p in range(2):
                    for w in range(2):
                        for j in range(3):
                            outer_taps(p, w, j)
                    if p == 0:
                        b, k = plan[("rc", NT - 1)]
                        dve.wait_ge(full[b], k)
                        dve.memset(v[:, :, :, HD:VW], 1.0).then_inc(ones_set, 1)
                        st.do(dve.memset(Cb[:, NT - 1, :, :], 0.0))
                        b, k = plan[("sp",)]
                        dve.wait_ge(free[b], k)
                    st.do(dve.memset(Cf[:, :, :], 0.0))
                    st.settle()
                    for i in range(NT - 1, 0, -1):
                        update_state(Cb[:, i - 1, :, :], Cb[:, i, :, :], ("cb0", p, i), ("cb1", p, i), p, 1, i)
                    for i in range(NT):
                        m = p * NT + i
                        dve.wait_ge(free[3], m + 1)
                        b, k = plan[("S", p, i)]
                        dve.wait_ge(full[b], k)
                        if m:
                            dve.wait_ge(full[7], m)
                        S = ps[b][:, 0:2 * P].rearrange("p (h t) -> p h t", h=2).unsqueeze(1).to_broadcast([P, 2, 2, P])
                        e4 = E.rearrange("p (d h t) -> p d h t", d=2, h=2)
                        dve.tensor_tensor(Pm.rearrange("p (d h t) -> p d h t", d=2, h=2), S, e4, ALU.mult).then_inc(free[b], 1)
                        update_state(Cf, Cf, ("cf0", p, i), ("cf1", p, i), p, 0, i)
                        for half in range(2):
                            dve.wait_ge(free[4 + half], m + 1)
                            dve.wait_ge(full[6 + half], m + 1)
                            q = slice(2 * half, 2 * half + 2)
                            dve.tensor_tensor(num[:, q, :], ps[6 + half][:, 0:2 * VW].rearrange("p (q d) -> p q d", q=2),
                                              inter[:, q, :], ALU.add).then_inc(free[6 + half], 1)
                        dve.wait_ge(free[7], m + 1)
                        den = num[:, :, HD]
                        st.do(dve.scalar_tensor_tensor(small[:, 0:4], den, -1.0, den, ALU.mult, ALU.max))
                        st.settle()
                        for half, d in ((0, 1), (1, 0)):
                            r = row(d, 2 * p)
                            st.do(dve.tensor_tensor(small[:, 4 + 2 * half:6 + 2 * half], small[:, 2 * half:2 * half + 2], cols[:, i, 2, r:r + 2], ALU.max))
                        st.settle()
                        st.do(dve.reciprocal(small[:, 8:12], small[:, 4:8]))
                        if m >= 2:
                            dve.wait_ge(hh_sq, 2 * (m - 1))
                            dve.wait_ge(y_raw, m - 1)
                        st.settle()
                        for h in range(2):
                            st.do(dve.tensor_scalar(hh[:, i % 2, h, :], num[:, h, 0:HD], small[:, 8 + h:9 + h], None, ALU.mult))
                        st.settle()
                        for h in range(2):
                            st.do(dve.scalar_tensor_tensor(hh[:, i % 2, h, :], num[:, 2 + h, 0:HD], small[:, 10 + h:11 + h],
                                                           hh[:, i % 2, h, :], ALU.mult, ALU.add))
                        st.settle()
                        dve.sem_inc(hh_ready, 1)
                    dve.wait_ge(hh_sq, 2 * (p + 1) * NT)
                    dve.tensor_scalar(ss_h[:, :], ss_h[:, :], 1.0 / HD, EPS, ALU.mult, ALU.add).then_inc(ms_ready, 1)
                    dve.wait_ge(rms_ready, p + 1)
                    dve.reciprocal(ss_h[:, :], ss_h[:, :]).then_inc(rs_ready, 1)

            @block.tensor
            def _(pe):
                def bank(key):
                    b, k = plan[key]
                    if k > 1:
                        pe.wait_ge(free[b], k - 1)
                    return b

                pe.wait_ge(ident_done, 1)
                for i in range(NT):
                    pe.wait_ge(xn_done, i + 1)
                    for h in range(2):
                        b = bank(("x", i, h))
                        for k in range(4):
                            c = (4 * h + k) * P
                            last = pe.transpose(ps[b][:, k * P:(k + 1) * P], xn[i % 2][:, c:c + P], ident[:, :])
                        last.then_inc(full[b], 1)
                pe.wait_ge(prow_in, 32)
                b = bank(("par",))
                pe.transpose(ps[b][:, 0:48], prow[0:48, :], ident[0:48, 0:48]).then_inc(full[b], 1)
                pe.wait_ge(gw_in, 64)
                b, k = plan[("x", NT - 1, 1)]
                pe.wait_ge(free[b], k)
                for i in range(NT + 1):
                    if i < NT:
                        b = bank(("g", i))
                        for k in range(KT):
                            last = pe.matmul(ps[b][:, 0:2 * NR], hT[:, k, tile_cols(i)], Wg[:, k, :], start=k == 0, stop=k == KT - 1)
                        last.then_inc(full[b], 1)
                    if i:
                        bg, kg = plan[("g", i - 1)]
                        pe.wait_ge(free[bg], kg)
                        b = bank(("gt", i - 1))
                        for r in range(2):
                            last = pe.transpose(ps[b][0:NR, r * P:(r + 1) * P], gtok[:, i - 1, r * NR:(r + 1) * NR], ident[:, :])
                        last.then_inc(full[b], 1)
                pe.wait_ge(w_slot_in[0], 16)
                for j in range(2):
                    for c, (lo, hi) in enumerate(CHUNKS):
                        b = bank(("u", j, c))
                        for k in range(KT):
                            last = pe.matmul(ps[b][:, 0:hi - lo], Wb[0][:, k, j * P:(j + 1) * P], hT[:, k, lo:hi], start=k == 0, stop=k == KT - 1)
                        last.then_inc(full[b], 1)

                def state_products(k0, k1, p, i, n, d):
                    read_out(pe, kw_key[n])
                    b0 = bank(k0)
                    s = n % 2
                    kwf = kw[:, s, :, :].rearrange("p h d -> p (h d)")
                    pe.matmul(ps[b0][:, 0:VW], kwf[:, 0:P], v[:, i, 0, :], start=True, stop=True)
                    pe.matmul(ps[b0][0:64, VW:2 * VW], kwf[:, P:HD], v[:, i, 0, :], start=True, stop=True)
                    pe.matmul(ps[b0][64:P, VW:2 * VW], kwf[:, HD:2 * P], v[:, i, 1, :], start=True, stop=True).then_inc(full[b0], 1)
                    b1 = bank(k1)
                    pe.matmul(ps[b1][:, 0:VW], kwf[:, 2 * P:3 * P], v[:, i, 1, :], start=True, stop=True).then_inc(full[b1], 1)

                def decay_exponents(p, i, n):
                    if n:
                        pe.wait_ge(free[3], n)
                    pe.matmul(ps[3][:, :], ident_b[:, :], masks[:, 1 if i == BT else 0, :, :].unsqueeze(2).to_broadcast([P, 2, 2, P]),
                              start=True, stop=False)
                    for q, (d, h) in enumerate(ORDER):
                        r = row(d, 2 * p + h)
                        last = pe.matmul(ps[3][:, q * P:(q + 1) * P], ident[0:NR, r:r + 1].to_broadcast([NR, P]),
                                         negM[0:NR, tile_cols(i)], start=False, stop=q == 3)
                    last.then_inc(full[3], 1)

                def queries(h, i):
                    c = tile_cols(i)
                    return ((qT[:, 0, c], 0), (qT[:, 1, c], 1)) if h == 0 else ((q1h[:, c], 1), (qT[:, 2, c], 2))

                def transpose_keys(key, i):
                    b = bank(key)
                    for j in range(3):
                        last = pe.transpose(ps[b][:, j * P:(j + 1) * P], kT[:, j, tile_cols(i)], ident[:, :])
                    last.then_inc(full[b], 1)

                pe.wait_ge(masks_done, 1)
                for p in range(2):
                    for w in range(2):
                        nb = 1 + 4 * p + w
                        pe.wait_ge(w_slot_in[nb % 2], 16 * (nb // 2 + 1))
                        for j in range(3):
                            for c, (lo, hi) in enumerate(CHUNKS):
                                b = bank(("qk", p, w, j, c))
                                for k in range(KT):
                                    last = pe.matmul(ps[b][:, 0:hi - lo], Wb[nb % 2][:, k, j * P:(j + 1) * P], hT[:, k, lo:hi],
                                                     start=k == 0, stop=k == KT - 1)
                                last.then_inc(full[b], 1)
                        if p == 0 and w == 0:
                            pe.wait_ge(pw_ready, 1)
                            for j in range(2):
                                pe.wait_ge(mixed_ready, j + 1)
                                src = mix0 if j == 0 else PA[:, 8:8 + T]
                                for g in range(3):
                                    b = bank(("po", j, g))
                                    for a in range(4 * g, min(4 * g + 4, NT)):
                                        c = (a - 4 * g) * P
                                        last = pe.matmul(ps[b][:, c:c + P], src[:, tile_cols(a)], pw[:, j, :], start=True, stop=True)
                                    last.then_inc(full[b], 1)
                    if p == 0:
                        pe.wait_ge(rows_ready, 1)
                        for i in range(NT):
                            b = bank(("rc", i))
                            for n, rr in enumerate((R[1], R[2], R[3], R[5])):
                                last = pe.transpose(ps[b][:, n * NR:(n + 1) * NR], rr[:, tile_cols(i)], ident[0:NR, 0:NR])
                            last.then_inc(full[b], 1)
                        b = bank(("sp",))
                        for pp in range(2):
                            for d in range(2):
                                for j in range(3):
                                    a = ((pp * 2 + d) * 3 + j) * NT
                                    for h in ((0,), (0, 1), (1,))[j]:
                                        parts = slice(0, P) if j != 1 else slice(64 * h, 64 * h + 64)
                                        n = P if j != 1 else 64
                                        r = row(d, 2 * pp + h)
                                        last = pe.matmul(ps[b][parts, a:a + NT], ident[0:NR, r:r + 1].to_broadcast([NR, n]),
                                                         S1[:, :], start=True, stop=True)
                        last.then_inc(full[b], 1)
                    for w in range(2):
                        nb = 3 + 4 * p + w
                        pe.wait_ge(w_slot_in[nb % 2], 16 * (nb // 2 + 1))
                        for i in range(NT):
                            b = bank(("vo", p, i, w))
                            for k in range(KT):
                                last = pe.matmul(ps[b][:, 0:PAIR], hT[:, k, tile_cols(i)], Wb[nb % 2][:, k, :], start=k == 0, stop=k == KT - 1)
                            last.then_inc(full[b], 1)
                    n = p * (2 * NT - 1)
                    pe.wait_ge(silu_done, 6 * (p + 1))
                    b, k = plan[("vo", p, NT - 1, 0)]
                    pe.wait_ge(free[b], k)
                    for i in range(NT - 1, 0, -1):
                        transpose_keys(("kb", p, i), i)
                        state_products(("cb0", p, i), ("cb1", p, i), p, i, n, 1)
                        n += 1
                    decay_exponents(p, 0, p * NT)
                    for i in range(NT):
                        m = p * NT + i
                        b = bank(("S", p, i))
                        for h in range(2):
                            for a, (q, j) in enumerate(queries(h, i)):
                                last = pe.matmul(ps[b][:, h * P:(h + 1) * P], kT[:, j, tile_cols(i)], q,
                                                 start=a == 0, stop=a == 1)
                        last.then_inc(full[b], 1)
                        transpose_keys(("kf", p, i), i)
                        for half, d in ((0, 1), (1, 0)):
                            if m:
                                pe.wait_ge(free[4 + half], m)
                            read_out(pe, ("cf1", p, i - 1) if d == 0 and i else ("cb1", p, 1))
                            for h in range(2):
                                for a, (q, j) in enumerate(queries(h, i)):
                                    C = Cb[:, i, j, :] if d == 1 else Cf[:, j, :]
                                    last = pe.matmul(ps[4 + half][:, h * VW:(h + 1) * VW], q, C,
                                                     start=a == 0, stop=a == 1)
                            last.then_inc(full[4 + half], 1)
                        if i + 1 < NT:
                            decay_exponents(p, i + 1, m + 1)
                        state_products(("cf0", p, i), ("cf1", p, i), p, i, n, 0)
                        n += 1
                        read_out(pe, ("S", p, i))
                        for half in range(2):
                            if m:
                                pe.wait_ge(free[6 + half], m)
                            for h in range(2):
                                q = 2 * half + h
                                last = pe.matmul(ps[6 + half][:, h * VW:(h + 1) * VW], Pm[:, q * P:(q + 1) * P], v[:, i, h, :],
                                                 start=True, stop=True)
                            last.then_inc(full[6 + half], 1)

        def slab(n, at=11 * D):
            return arena[:, at + n * D:at + (n + 1) * D]

        y_t, x_t, yT_t, x2, t_t, tT_t = ([slab(2 * n + s) for s in range(2)] for n in range(6))
        g2b = arena[:, 8 * D:9 * D]
        wr = arena[:, 9 * D:9 * D + KT * NE].rearrange("p (k e) -> p k e", k=KT)
        L = arena[:, 9 * D + 128:9 * D + 128 + NT * NE].rearrange("p (i e) -> p i e", i=NT)
        AF = arena[0:NE, 9600:9600 + T]
        RING = 23 * D
        ring = [arena[:, RING + s * 4096:RING + (s + 1) * 4096].rearrange("p (k n) -> p k n", k=KT) for s in range(6)]
        vals = arena[0:NE, 48 * D:48 * D + 176]
        inds = arena[0:NE, 48 * D + 176:48 * D + 352].bitcast(U32)
        ranked = arena[0:NE, 48 * D + 352:48 * D + 352 + 2 * SLOTS].rearrange("p (w s) -> p w s", w=2)
        smx = sb("smx", [P, NT])
        idxc = sb("idxc", [P, 2, NE], U32)
        gatec = sb("gatec", [P, 2, NE])
        slot_in = [sem(f"ring{s}_in") for s in range(6)]
        y_in = [sem("y_in0"), sem("y_in1")]
        x3_in = [sem("x3_in0"), sem("x3_in1")]
        x3_clear, g2_in, wr_in = sem("x3_clear"), sem("g2_in"), sem("wr_in")
        x2_ready, x2_sq, t_ready = sem("x2_ready"), sem("x2_sq"), sem("t_ready")
        x2_out = [sem("x2_out0"), sem("x2_out1")]
        t_out = [sem("t_out0"), sem("t_out1")]
        soft_dve, soft_act, aff_ready = sem("soft_dve"), sem("soft_act"), sem("aff_ready")
        topk_step, ranked_ready, idx_ready = sem("topk_step"), sem("ranked_ready"), sem("idx_ready")

        def expert_source(slot, e):
            w = (w_gate, w_up, w_gate, w_up, w_down, w_down)[slot]
            half = (0, 0, 1, 1, 0, 1)[slot]
            return w[0][e, :, half * 512:(half + 1) * 512].rearrange("a (k p) n -> p (a k) n", p=P)

        with nc.Block() as block:
            @block.sync
            def _(sp):
                sp.dma_start(g2b, g2[0:1, :].to_broadcast([P, D])).then_inc(g2_in, 16)
                sp.dma_start(wr, w_router[0].rearrange("(k p) e -> p k e", p=P)).then_inc(wr_in, 16)

                def load(i):
                    if i >= 2:
                        multiplied(sp, ("yT", i - 2, 1))
                    sp.dma_start(y_t[i % 2], y_d[i * P:(i + 1) * P, :]).then_inc(y_in[i % 2], 16)
                    if i in (0, BT):
                        sp.wait_ge(x3_clear, 1 if i == 0 else 2)
                    if i >= 2:
                        read_out(sp, ("wo", i - 2, 1))
                    for p0, src in x_rows[i]:
                        sp.dma_start(x_t[i % 2][p0:p0 + src.shape[0], :], src).then_inc(x3_in[i % 2], 16)

                load(0)
                load(1)
                for s in range(6):
                    sp.dma_start(ring[s], expert_source(s, slice(0, 1))).then_inc(slot_in[s], 16)
                for i in range(NT):
                    if i + 2 < NT:
                        load(i + 2)
                    sp.wait_ge(x2_ready, 2 * (i + 1))
                    sp.dma_start(acc_d[i * P:(i + 1) * P, :], x2[i % 2]).then_inc(x2_out[i % 2], 16)
                    sp.wait_ge(t_ready, i + 1)
                    sp.dma_start(t_d[i * P:(i + 1) * P, :], t_t[i % 2]).then_inc(t_out[i % 2], 16)
                for s in range(2):
                    n = 16 * len(range(s, NT, 2))
                    sp.wait_ge(x2_out[s], n)
                    sp.wait_ge(t_out[s], n)

            @block.scalar
            def _(act):
                st = Steps(act, sem("act_step_b"))

                def quad(ap):
                    return ap.rearrange("p (k t) -> p k t", k=4)

                def move(key, out):
                    multiplied(act, key)
                    act.activation(out, ps[plan[key][0]][:, :], ACT.Copy).then_inc(free[plan[key][0]], 1)

                def y_transposed(i):
                    if i >= 2:
                        multiplied(act, ("wo", i - 2, 1))
                    for h in range(2):
                        move(("yT", i, h), yT_t[i % 2][:, 512 * h:512 * h + 512])

                y_transposed(0)
                for i in range(NT + 1):
                    if i < NT:
                        if i + 1 < NT:
                            y_transposed(i + 1)
                        act.wait_ge(x2_ready, 2 * (i + 1))
                        if i:
                            st.settle()
                        st.do(act.activation(junk_b, x2[i % 2], ACT.Square, accum_out=small[:, i:i + 1]))
                        st.settle()
                        st.do(act.activation(small[:, 16 + i:17 + i], small[:, i:i + 1], ACT.Copy, scale=1.0 / D, bias=EPS))
                        st.settle()
                        act.activation(small[:, 32 + i:33 + i], small[:, 16 + i:17 + i], ACT.Sqrt).then_inc(x2_sq, 1)
                    if i:
                        for h in range(2):
                            move(("tT", i - 1, h), tT_t[(i - 1) % 2][:, 512 * h:512 * h + 512])
                        multiplied(act, ("lg", i - 1))
                        b = plan[("lg", i - 1)][0]
                        act.activation(L[:, i - 1, :], ps[b][:, 0:NE], ACT.Copy).then_inc(free[b], 1)
                act.wait_ge(soft_dve, 1)
                act.activation(L, L, ACT.Exp).then_inc(soft_act, 1)
                for g in range(3):
                    multiplied(act, ("af", g))
                    b = plan[("af", g)][0]
                    w = 512 if g < 2 else T - 1024
                    act.activation(AF[:, 512 * g:512 * g + w], ps[b][0:NE, 0:w], ACT.Copy).then_inc(free[b], 1)

            @block.vector
            def _(dve):
                st = Steps(dve, topk_step)
                dve.memset(x_t[0][0:64, :], 0.0).then_inc(x3_clear, 1)
                for i in range(NT):
                    if i == BT:
                        read_out(dve, ("wo", 0, 1))
                        dve.memset(x_t[0][64:P, :], 0.0).then_inc(x3_clear, 1)
                    n = 16 * sum(len(x_rows[a]) for a in range(i % 2, i + 1, 2))
                    dve.wait_ge(x3_in[i % 2], n)
                    if i >= 2:
                        dve.wait_ge(x2_out[i % 2], 16 * (i // 2))
                        dve.wait_ge(t_out[i % 2], 16 * (i // 2))
                        multiplied(dve, ("tT", i - 2, 1))
                    for h in range(2):
                        multiplied(dve, ("wo", i, h))
                        b = plan[("wo", i, h)][0]
                        c = slice(512 * h, 512 * h + 512)
                        dve.tensor_tensor(x2[i % 2][:, c], ps[b][:, :], x_t[i % 2][:, c], ALU.add).then_inc(free[b], 1)
                        read_out(dve, ("wo", i, h))
                        dve.sem_inc(x2_ready, 1)
                    dve.wait_ge(x2_sq, i + 1)
                    st.do(dve.reciprocal(small[:, 48 + i:49 + i], small[:, 32 + i:33 + i]))
                    if i == 0:
                        dve.wait_ge(g2_in, 16)
                    st.settle()
                    dve.scalar_tensor_tensor(t_t[i % 2], x2[i % 2], small[:, 48 + i:49 + i], g2b, ALU.mult, ALU.mult).then_inc(t_ready, 1)
                read_out(dve, ("lg", NT - 1))
                st.do(dve.tensor_reduce(smx[:, :], L, AX.X, ALU.max))
                st.settle()
                dve.tensor_tensor(L, L, smx[:, :].unsqueeze(2).to_broadcast([P, NT, NE]), ALU.subtract).then_inc(soft_dve, 1)
                dve.wait_ge(soft_act, 1)
                st.do(dve.tensor_reduce(smx[:, :], L, AX.X, ALU.add))
                st.settle()
                st.do(dve.reciprocal(smx[:, :], smx[:, :]))
                st.settle()
                dve.tensor_tensor(L, L, smx[:, :].unsqueeze(2).to_broadcast([P, NT, NE]), ALU.mult).then_inc(aff_ready, 1)
                for s, (cap, at) in ((0, (CAP_P, 136)), (1, (CAP_S, 0))):
                    lo, hi = REAL[s]
                    rounds = -(-cap // 8)
                    for g in range(3):
                        read_out(dve, ("af", g))
                    for r in range(rounds):
                        c = slice(at + 8 * r, at + 8 * r + 8)
                        st.do(dve.max(vals[:, c], AF[:, lo:hi]))
                        st.settle()
                        st.do(dve.max_index(inds[:, c], vals[:, c], AF[:, lo:hi]))
                        if r + 1 < rounds:
                            st.do(dve.match_replace(AF[:, lo:hi], vals[:, c], AF[:, lo:hi], -1.0))
                            st.settle()
                st.settle()
                for (a, b), (c, d), base in (((0, CAP_S), (0, CAP_S), REAL[1][0]), ((CAP_S, SLOTS), (136, 136 + CAP_P), REAL[0][0])):
                    st.do(dve.tensor_scalar(ranked[:, 0, a:b], inds[:, c:d], float(base), None, ALU.add))
                    st.do(dve.tensor_copy(ranked[:, 1, a:b], vals[:, c:d]))
                st.settle()
                dve.sem_inc(ranked_ready, 1)
                multiplied(dve, ("ix",))
                b = plan[("ix",)][0]
                for blk, n in ((0, P), (1, SB_ROWS)):
                    st.do(dve.tensor_copy(idxc[0:n, blk, 0:NE], ps[b][0:n, (2 * blk) * NE:(2 * blk + 1) * NE]))
                    st.do(dve.tensor_copy(gatec[0:n, blk, :], ps[b][0:n, (2 * blk + 1) * NE:(2 * blk + 2) * NE]))
                st.settle()

            @block.tensor
            def _(pe):
                def bank(key):
                    b, k = plan[key]
                    if k > 1:
                        pe.wait_ge(free[b], k - 1)
                    return b

                def transposes(name, i, src):
                    for h in range(2):
                        b = bank((name, i, h))
                        for k in range(4):
                            c = (4 * h + k) * P
                            last = pe.transpose(ps[b][:, k * P:(k + 1) * P], src[:, c:c + P], ident[:, :])
                        last.then_inc(full[b], 1)

                pe.wait_ge(y_in[0], 16)
                transposes("yT", 0, y_t[0])
                pe.wait_ge(wout_in, 16)
                for i in range(NT + 1):
                    if i < NT:
                        for h in range(2):
                            if h == 0:
                                read_out(pe, ("yT", i, 1))
                            b = bank(("wo", i, h))
                            for k in range(KT):
                                last = pe.matmul(ps[b][:, :], yT_t[i % 2][:, k * P:(k + 1) * P], wout[:, k, 512 * h:512 * h + 512],
                                                 start=k == 0, stop=k == KT - 1)
                            last.then_inc(full[b], 1)
                        if i + 1 < NT:
                            pe.wait_ge(y_in[(i + 1) % 2], 16 * ((i + 1) // 2 + 1))
                            transposes("yT", i + 1, y_t[(i + 1) % 2])
                    if i:
                        pe.wait_ge(t_ready, i)
                        transposes("tT", i - 1, t_t[(i - 1) % 2])
                        if i == 1:
                            pe.wait_ge(wr_in, 16)
                        read_out(pe, ("tT", i - 1, 1))
                        b = bank(("lg", i - 1))
                        for k in range(KT):
                            last = pe.matmul(ps[b][:, 0:NE], tT_t[(i - 1) % 2][:, k * P:(k + 1) * P], wr[:, k, :], start=k == 0, stop=k == KT - 1)
                        last.then_inc(full[b], 1)
                pe.wait_ge(aff_ready, 1)
                for g in range(3):
                    b = bank(("af", g))
                    for i in range(4 * g, min(4 * g + 4, NT)):
                        last = pe.transpose(ps[b][0:NE, (i - 4 * g) * P:(i - 4 * g + 1) * P], L[:, i, :], ident[:, :])
                    last.then_inc(full[b], 1)
                pe.wait_ge(ranked_ready, 1)
                b = bank(("ix",))
                for blk, (lo, hi) in enumerate(((0, P), (P, SLOTS))):
                    for w in range(2):
                        c = (2 * blk + w) * NE
                        last = pe.transpose(ps[b][0:hi - lo, c:c + NE], ranked[:, w, lo:hi], ident[0:NE, 0:NE])
                last.then_inc(full[b], 1)

        xe = arena[:, 0:2 * D].rearrange("p (b n) -> p b n", b=2)
        xeT = arena[:, 2048:2048 + KT * SLOTS].rearrange("p (k s) -> p k s", k=KT)
        hidT = arena[:, 3360:3360 + KT * SLOTS].rearrange("p (k s) -> p k s", k=KT)
        sil = arena[:, 4672:4672 + 4 * SLOTS].rearrange("p (b f s) -> p b f s", b=2, f=2)
        yeT = arena[:, 5328:5328 + KT * SLOTS].rearrange("p (k s) -> p k s", k=KT)
        yeS = arena[:, 6640:6640 + 2 * D].rearrange("p (b n) -> p b n", b=2)
        cur_gather = sb("cur_gather", [P, 2, 1], U32)
        cur_scatter = sb("cur_scatter", [P, 2, 1], U32)
        gu_full, sil_done, hid_done = sem("gu_full"), sem("sil_done"), sem("hid_done")
        dn_full, dn_done = sem("dn_full"), sem("dn_done")
        t_full, t_done = sem("t_full"), sem("t_done")
        o_full, o_done = sem("o_full"), sem("o_done")
        xe_in, acc_out, ye_free, idx_step = sem("xe_in"), sem("acc_out"), sem("ye_free"), sem("idx_step")
        passed, passed_pe = sem("passed"), sem("passed_pe")
        BLKS = ((0, P), (1, SB_ROWS))

        def pair_of_tiles(b):
            return ps[b][:, 0:2 * SLOTS].rearrange("p (f s) -> p f s", f=2)

        with nc.Block() as block:
            @block.sync
            def _(sp):
                with sp.Fori(0, NE - 1) as i:
                    for s in range(6):
                        done = (gu_full, 2) if s < 2 else (gu_full, 4) if s < 4 else (dn_full, 2 * (s - 3))
                        sp.wait_ge(done[0], i * 4 + done[1])
                        sp.dma_start(ring[s], expert_source(s, bass.ds(i + 1, 1))).then_inc(slot_in[s], 16)

            @block.gpsimd
            def _(pool):
                def gather(e, n_steps):
                    at = bass.ds(e, 1)
                    for blk, n in BLKS:
                        pool.tensor_copy(cur_gather[0:n, blk, :], idxc[0:n, blk, at]).then_inc(idx_step, 1)
                    pool.wait_ge(idx_step, n_steps + 2)
                    pool.sem_inc(passed, 1)
                    for blk, n in BLKS:
                        pool.indirect_dma_start(out=xe[0:n, blk, :], out_offset=None, in_=t_d[:, :],
                                                in_offset=bass.IndirectOffsetOnAxis(ap=cur_gather[0:n, blk, :], axis=0)).then_inc(xe_in, 16)

                def scatter(e, n_steps):
                    at = bass.ds(e, 1)
                    for blk, n in BLKS:
                        pool.tensor_copy(cur_scatter[0:n, blk, :], idxc[0:n, blk, at]).then_inc(idx_step, 1)
                    pool.wait_ge(idx_step, n_steps + 2)
                    pool.sem_inc(passed, 1)
                    pool.wait_ge(o_done, e * 4 + 5)
                    pool.sem_inc(passed, 1)
                    for blk, n in BLKS:
                        pool.indirect_dma_start(out=acc_d[:, :], out_offset=bass.IndirectOffsetOnAxis(ap=cur_scatter[0:n, blk, :], axis=0),
                                                in_=yeS[0:n, blk, :], in_offset=None, compute_op=ALU.add).then_inc(acc_out, 16)
                    pool.wait_ge(acc_out, e * 32 + 32)
                    pool.sem_inc(ye_free, 1)

                pool.sem_inc(ye_free, 1)
                gather(0, 0)
                pool.wait_ge(t_full, 4)
                gather(1, 2)
                with pool.Fori(0, NE - 2) as i:
                    pool.wait_ge(t_full, i * 4 + 8)
                    pool.sem_inc(passed, 1)
                    gather(i + 2, i * 4 + 4)
                    scatter(i, i * 4 + 6)
                pool.wait_ge(xe_in, 32 * NE)
                for e in (NE - 2, NE - 1):
                    scatter(e, 4 * (NE - 1) + 2 * (e - NE + 1) + 2)

            @block.scalar
            def _(act):
                def silu(e):
                    for fp in range(4):
                        act.wait_ge(gu_full, e * 4 + fp + 1)
                        act.wait_ge(hid_done, e * 4 + fp + 1)
                        act.activation(sil[:, fp % 2, :, :], pair_of_tiles(fp % 2), ACT.Silu).then_inc(sil_done, 1)

                def results(e):
                    for dp in range(4):
                        act.wait_ge(dn_full, e * 4 + dp + 1)
                        act.activation(yeT[:, 2 * dp:2 * dp + 2, :], pair_of_tiles(4 + dp % 2), ACT.Copy).then_inc(dn_done, 1)

                act.sem_inc(dn_done, 2)
                silu(0)
                with act.Fori(0, NE - 1) as i:
                    results(i)
                    silu(i + 1)
                results(NE - 1)

            @block.vector
            def _(dve):
                def move_rows(e):
                    for m in range(4):
                        dve.wait_ge(t_full, e * 4 + m + 1)
                        dve.tensor_copy(xeT[:, 2 * m:2 * m + 2, :], pair_of_tiles(6)).then_inc(t_done, 1)

                def hidden(e, fp):
                    dve.wait_ge(sil_done, e * 4 + fp + 1)
                    dve.tensor_tensor(hidT[:, 2 * fp:2 * fp + 2, :], pair_of_tiles(2 + fp % 2), sil[:, fp % 2, :, :], ALU.mult).then_inc(hid_done, 1)

                def scaled(e, m):
                    h, (blk, n) = m // 2, BLKS[m % 2]
                    if m == 0:
                        dve.wait_ge(ye_free, e + 1)
                    dve.wait_ge(o_full, e * 4 + m + 1)
                    dve.tensor_scalar(yeS[0:n, blk, 512 * h:512 * h + 512], ps[7][0:n, :], gatec[0:n, blk, bass.ds(e, 1)], None,
                                      ALU.mult).then_inc(o_done, 1)

                dve.sem_inc(hid_done, 2)
                dve.sem_inc(o_done, 1)
                move_rows(0)
                for fp in range(4):
                    hidden(0, fp)
                with dve.Fori(0, NE - 1) as i:
                    move_rows(i + 1)
                    for m in range(4):
                        hidden(i + 1, m)
                        scaled(i, m)
                for m in range(4):
                    scaled(NE - 1, m)

            @block.tensor
            def _(pe):
                def transpose_rows(e, m, first=False):
                    if not first:
                        pe.wait_ge(t_done, e * 4 + m)
                    for a in range(2):
                        k = 2 * m + a
                        for (blk, n), c in zip(BLKS, (0, P)):
                            last = pe.transpose(ps[6][:, a * SLOTS + c:a * SLOTS + c + n], xe[0:n, blk, k * P:(k + 1) * P], ident[0:n, 0:n])
                    last.then_inc(t_full, 1)

                def gate_up(e, fp):
                    if fp == 0:
                        pe.wait_ge(t_done, e * 4 + 4)
                    if fp % 2 == 0:
                        for s in (fp, fp + 1):
                            pe.wait_ge(slot_in[s], e * 16 + 16)
                    pe.wait_ge(hid_done, e * 4 + fp + 1)
                    for w in range(2):
                        for a in range(2):
                            f = (2 * fp + a) % 4
                            for k in range(KT):
                                last = pe.matmul(ps[2 * w + fp % 2][:, a * SLOTS:(a + 1) * SLOTS], ring[2 * (fp // 2) + w][:, k, f * P:(f + 1) * P],
                                                 xeT[:, k, :], start=k == 0, stop=k == KT - 1)
                    last.then_inc(gu_full, 1)

                def down(e, dp):
                    if dp % 2 == 0:
                        pe.wait_ge(slot_in[4 + dp // 2], e * 16 + 16)
                    if dp == 0:
                        pe.wait_ge(hid_done, e * 4 + 5)
                    pe.wait_ge(dn_done, e * 4 + dp + 1)
                    for a in range(2):
                        dt = (2 * dp + a) % 4
                        for k in range(KT):
                            if dp == 0 and a == 0 and k == 6:
                                pe.wait_ge(hid_done, e * 4 + 6)
                            last = pe.matmul(ps[4 + dp % 2][:, a * SLOTS:(a + 1) * SLOTS], ring[4 + dp // 2][:, k, dt * P:(dt + 1) * P],
                                             hidT[:, k, :], start=k == 0, stop=k == KT - 1)
                    last.then_inc(dn_full, 1)

                def transpose_results(e, m):
                    h, (blk, n) = m // 2, BLKS[m % 2]
                    pe.wait_ge(dn_done, e * 4 + 2 * h + 4)
                    pe.wait_ge(o_done, e * 4 + m + 1)
                    if blk:
                        pe.sem_inc(passed_pe, 1)
                    for k in range(4):
                        last = pe.transpose(ps[7][0:n, k * P:(k + 1) * P], yeT[:, 4 * h + k, blk * P:blk * P + n], ident[:, :])
                    last.then_inc(o_full, 1)

                pe.wait_ge(xe_in, 32)
                for m in range(4):
                    transpose_rows(0, m, first=m == 0)
                for fp in range(4):
                    gate_up(0, fp)
                with pe.Fori(0, NE - 1) as i:
                    pe.wait_ge(xe_in, i * 32 + 64)
                    for m in range(4):
                        transpose_rows(i + 1, m)
                        down(i, m)
                    for m in range(4):
                        gate_up(i + 1, m)
                        transpose_results(i, m)
                for m in range(4):
                    down(NE - 1, m)
                    if m == 2:
                        transpose_results(NE - 1, 0)
                        transpose_results(NE - 1, 1)
                for m in (2, 3):
                    transpose_results(NE - 1, m)

        fin = [arena[:, 11 * D + i * D:12 * D + i * D] for i in range(NT)]
        fgb = arena[:, 22 * D:23 * D]
        fin_in = [sem(f"fin{i}_in") for i in range(NT)]
        fg_in, fin_sq, fin_ready, y_stored = sem("fg_in"), sem("fin_sq"), sem("fin_ready"), sem("y_stored")
        outs = {0: [(64, y_prompt[0, 0:64, :])], 1: [(0, y_prompt[0, 64:192, :])], 2: [(0, y_prompt[0, 192:256, :])]}
        for i in range(3, NT):
            outs[i] = [(0, y_sample[0, (i - 3) * P:(i - 2) * P, :])]
        with nc.Block() as block:
            @block.sync
            def _(sp):
                sp.dma_start(fgb, final_g.rearrange("(a n) -> a n", a=1).to_broadcast([P, D])).then_inc(fg_in, 16)
                for i in range(NT):
                    sp.dma_start(fin[i], acc_d[i * P:(i + 1) * P, :]).then_inc(fin_in[i], 16)
                for i in range(NT):
                    sp.wait_ge(fin_ready, i + 1)
                    for p0, dst in outs[i]:
                        sp.dma_start(dst, fin[i][p0:p0 + dst.shape[0], :]).then_inc(y_stored, 16)
                sp.wait_ge(y_stored, 16 * NT)

            @block.scalar
            def _(act):
                st = Steps(act, sem("act_step_d"))
                for i in range(NT):
                    act.wait_ge(fin_in[i], 16)
                    if i:
                        st.settle()
                    st.do(act.activation(junk_b, fin[i], ACT.Square, accum_out=small[:, i:i + 1]))
                    st.settle()
                    st.do(act.activation(small[:, 16 + i:17 + i], small[:, i:i + 1], ACT.Copy, scale=1.0 / D, bias=EPS))
                    st.settle()
                    act.activation(small[:, 32 + i:33 + i], small[:, 16 + i:17 + i], ACT.Sqrt).then_inc(fin_sq, 1)

            @block.vector
            def _(dve):
                st = Steps(dve, sem("dve_step_d"))
                dve.wait_ge(fg_in, 16)
                for i in range(NT):
                    dve.wait_ge(fin_sq, i + 1)
                    st.do(dve.reciprocal(small[:, 48 + i:49 + i], small[:, 32 + i:33 + i]))
                    st.settle()
                    dve.scalar_tensor_tensor(fin[i], fin[i], small[:, 48 + i:49 + i], fgb, ALU.mult, ALU.mult).then_inc(fin_ready, 1)


_INS = ("x_prompt", "x_sample", "meta_tokens", "norm1_g", "w_in", "conv_w", "conv_b", "gate_b", "pool_w", "pool_scale",
        "mh_norm_g", "w_out", "norm2_g", "w_router", "w_gate", "w_up", "w_down", "final_g")


def window_reciprocals():
    out = np.ones((4, T), np.float32)
    for g, w in enumerate((2, 4, 8, 16)):
        for lo, hi in REAL:
            t = np.arange(hi - lo)
            n = np.clip(t - w // 2 + w, 0, hi - lo) - np.clip(t - w // 2, 0, hi - lo)
            out[g, lo:hi] = np.float32(1.0) / n.astype(np.float32)
    return out


def kernel(**inputs):
    import concourse.bacc as bacc
    from concourse.bass_utils import run_bass_kernel_spmd

    nc = bacc.Bacc("TRN2", target_bir_lowering=False, num_devices=1)
    arrays = {f"in_{n}": np.ascontiguousarray(inputs[n]) for n in _INS}
    arrays["window_reciprocals"] = window_reciprocals()
    args = [nc.dram_tensor(n, a.shape, mybir.dt.from_np(a.dtype), kind="ExternalInput").ap() for n, a in arrays.items()]
    outs = [nc.dram_tensor(n, (1, rows, D), F32, kind="ExternalOutput").ap()
            for n, rows in (("y_prompt", SEQ_P), ("y_sample", SEQ_S))]
    encoder_program(nc, *args, *outs)
    r = run_bass_kernel_spmd(nc, [arrays], core_ids=[0])
    return r.results[0]["y_prompt"], r.results[0]["y_sample"]
```

```python
import math

import numpy as np
import concourse.bass as bass
from concourse import mybir
from concourse.alu_op_type import AluOpType as ALU
from contextlib import ExitStack

F32 = mybir.dt.float32
BF16 = mybir.dt.bfloat16
U32 = mybir.dt.uint32
ACT = mybir.ActivationFunctionType
AX = mybir.AxisListType

P = 128
D = 1024
KT = D // P
N_META, PAD = 16, 48
SEQ_P, SEQ_S = 256, 1024
BOUND = PAD + N_META + SEQ_P
T = BOUND + PAD + N_META + SEQ_S
NT = T // P
BT = BOUND // P
REAL = ((PAD, BOUND), (BOUND + PAD, T))
D_POOL, D_ML = 256, 768
HD = 192
PAIR = 2 * HD
VW = HD + 1
NE = 16
Y_W = D_POOL + PAIR
CAP_P, CAP_S = 2 * 272 // NE, 2 * 1040 // NE
SLOTS = CAP_P + CAP_S
SB_ROWS = SLOTS - P
EPS = 1e-6
NEG = -1e30
LN_SCALE = math.log(HD ** -0.5)
ORDER_X = (1, 3, 0, 2) + tuple(range(4, NT))
ORDER_B = tuple(range(BT, NT)) + tuple(range(BT))
SPLIT = 8
STEP_A, STEP_B = SPLIT - BT, NT - BT
CHUNKS = ((0, 512), (512, 1024), (1024, T))
BW = 32
NR = BW + 4


def layout():
    o, at = {}, 0
    for name, n in (("hT", KT * T), ("qT", 3 * T), ("kT", 3 * 1424), ("og", NT * PAIR), ("v", NT * 2 * VW + 2),
                    ("Cb", NT * 3 * VW + 1), ("W", 2 * KT * PAIR), ("Z", 1424), ("negM", T), ("E", 512),
                    ("Pm", 512), ("inter", 4 * VW), ("num", 4 * VW), ("kw", 2 * PAIR), ("Cf", 3 * VW + 1),
                    ("hh", 2 * PAIR), ("mhg", PAIR), ("q1h", T), ("pw", 2 * P), ("junk", HD)):
        o[name] = at
        at += n
    o["end"] = at
    return o


def bank_plan():
    keys = []
    for i in range(NT):
        keys += [("x", i, 0), ("x", i, 1)]
    keys += [("par",)]
    for i in range(NT + 1):
        if i < NT:
            keys.append(("g", i))
        if i:
            keys.append(("gt", i - 1))
    keys += [("u", j, c) for j in range(2) for c in range(3)]
    for p in range(2):
        keys += [("qk", p, 0, j, c) for j in range(3) for c in range(3)]
        keys += [("vo", p, i, 1) for i in range(NT)]
        if p == 0:
            keys += [("rc", i) for i in range(NT)] + [("sp",)]
            keys += [("po", j, g) for j in range(2) for g in range(3)]
        keys += [("qk", p, 1, j, c) for j in range(3) for c in range(3)]
        keys += [("vo", p, i, 0) for i in range(NT)]
        keys += [("kb", p, NT - 1)]
        for i in range(NT - 1, 0, -1):
            keys += [("kb", p, i - 1)] if i > 1 else []
            keys += [("cb0", p, i), ("cb1", p, i)]
        for i in range(NT):
            keys += [("S", p, i), ("kf", p, i), ("cf0", p, i), ("cf1", p, i)]
    keys += [("yT", 0, 0), ("yT", 0, 1)]
    for n in range(NT):
        keys.append(("wo", n, 0))
        if n:
            keys += [("tT", n - 1, 0), ("tT", n - 1, 1)]
        if n + 1 < NT:
            keys += [("yT", n + 1, 0), ("yT", n + 1, 1)]
        if n:
            keys.append(("lg", n - 1))
        keys.append(("wo", n, 1))
        keys += {STEP_A: [("af", 0), ("af", 1)], STEP_B: [("af", 2)]}.get(n, [])
    keys += [("tT", NT - 1, 0), ("tT", NT - 1, 1), ("lg", NT - 1), ("af", 3), ("ix",)]
    plan, used = {}, [0, 0, 0]
    for n, key in enumerate(keys):
        used[n % 3] += 1
        plan[key] = (n % 3, used[n % 3])
    return plan


class Steps:

    def __init__(self, eng, sem):
        self.eng, self.sem, self.n = eng, sem, 0

    def do(self, ins):
        ins.then_inc(self.sem, 1)
        self.n += 1
        return self.n

    def settle(self):
        self.eng.wait_ge(self.sem, self.n)


def encoder_program(nc, x_prompt, x_sample, meta, g1, w_in, conv_w, conv_b, gate_b, pool_w, pool_scale,
                    mh_g, w_out, g2, w_router, w_gate, w_up, w_down, final_g, rcount, y_prompt, y_sample):
    plan, off = bank_plan(), layout()
    y_d = nc.dram_tensor("mixer_out", (T, Y_W), F32, kind="Internal").ap()
    t_d = nc.dram_tensor("ffn_in", (T, D), F32, kind="Internal").ap()
    acc_d = nc.dram_tensor("residual", (T, D), F32, kind="Internal").ap()

    ctx = ExitStack()
    with ctx:
        def sb(name, shape, dt=F32):
            return ctx.enter_context(nc.sbuf_tensor(name, shape, dt))

        def sem(name):
            return ctx.enter_context(nc.semaphore(name))

        arena = sb("arena", [P, off["end"]])

        def area(name, n, parts=P, shift=0):
            a = off[name] + shift if isinstance(name, str) else name + shift
            return arena[0:parts, a:a + n]

        ident = sb("ident", [P, P])
        ident_b = sb("ident_b", [P, P], BF16)
        masks = sb("masks", [P, 2, 2, P], BF16)
        cols = sb("cols", [P, NT, 4, NR])
        spc = sb("spc", [P, 12, NT])
        par = sb("par", [P, 56])
        small = sb("small", [P, 96])
        ss_h = sb("ss_h", [P, 2 * NT])
        gb = sb("gb", [NR, 2])
        S0 = sb("S0", [NR, NT])
        S1 = sb("S1", [NR, NT])
        ps = [ctx.enter_context(nc.psum_tensor(f"bank{b}", [P, 512], F32)) for b in range(8)]

        hT = area("hT", KT * T).rearrange("p (k t) -> p k t", k=KT)
        qT = area("qT", 3 * T).rearrange("p (j t) -> p j t", j=3)
        kT = area("kT", 3 * T).rearrange("p (j t) -> p j t", j=3)
        qkT = (qT, kT)
        q1h = area("q1h", T)
        og = area("og", NT * PAIR).rearrange("p (i h d) -> p i h d", i=NT, h=2)
        v = area("v", NT * 2 * VW).rearrange("p (i h d) -> p i h d", i=NT, h=2)
        Cb = area("Cb", NT * 3 * VW).rearrange("p (i j d) -> p i j d", i=NT, j=3)
        Cf = area("Cf", 3 * VW).rearrange("p (j d) -> p j d", j=3)
        Wb = [area("W", KT * PAIR, shift=s * KT * PAIR).rearrange("p (k n) -> p k n", k=KT) for s in range(2)]
        Z = area("Z", 1424)
        negM = area("negM", T, NR)
        E = area("E", 512)
        Pm = area("Pm", 512)
        inter = area("inter", 4 * VW).rearrange("p (q d) -> p q d", q=4)
        num = area("num", 4 * VW).rearrange("p (q d) -> p q d", q=4)
        kw = area("kw", 2 * PAIR).rearrange("p (s h d) -> p s h d", s=2, h=2)
        hh = area("hh", 2 * PAIR).rearrange("p (s h d) -> p s h d", s=2, h=2)
        mhg = area("mhg", PAIR)
        Wg = area("kw", KT * 2 * NR).rearrange("p (k n) -> p k n", k=KT)
        pw = area("pw", 2 * P).rearrange("p (j n) -> p j n", j=2)
        psc = area("Cf", 2 * P).rearrange("p (j n) -> p j n", j=2)
        xin = [area("og", D, shift=i * D) for i in range(4)] + [area("v", D, shift=i * D) for i in range(NT - 4)]
        xn = [area("qT", D, shift=(2 + s) * D) for s in range(2)]
        g1b = area("kT", D)
        gtok = area("Z", NT * 2 * NR).rearrange("p (i n) -> p i n", i=NT)
        prow = area("E", P, 48)
        R = [area("v", T, NR, shift=n * T) for n in range(7)]
        R01 = area("v", 2 * T, NR).rearrange("p (r t) -> p r t", r=2)
        U, PA, PB = (area("kT", 1424, shift=n * 1424) for n in range(3))
        rc_t = area("E", T)
        mix0 = area("E", T, shift=T)
        ypool = [area("kT", T, shift=n * 1424) for n in (0, 2)]
        junk_h = area("junk", HD)
        wout = area(0, KT * D).rearrange("p (k n) -> p k n", k=KT)
        wout_in = sem("wout_in")
        junk_b = area(47 * D, D)

        full = [sem(f"bank{b}_full") for b in range(8)]
        free = [sem(f"bank{b}_free") for b in range(8)]
        x_in = [sem(f"x_in{i}") for i in range(NT)]
        x_clear = sem("x_clear")
        sq_done = sem("sq_done")
        xn_done = sem("xn_done")
        params_in = sem("params_in")
        prow_in, gw_in, gb_in = sem("prow_in"), sem("gw_in"), sem("gb_in")
        pool_par_in, mhg_in = sem("pool_par_in"), sem("mhg_in")
        zeroed = sem("zeroed")
        ident_done = sem("ident_done")
        masks_done = sem("masks_done")
        w_slot_in = [sem("w_slot0_in"), sem("w_slot1_in")]
        act_step, dve_step, pool_step = sem("act_step"), sem("dve_step"), sem("pool_step")
        rows_dve = sem("rows_dve")
        rows_act = sem("rows_act")
        rows_ready = sem("rows_ready")
        mixed_ready = sem("mixed_ready")
        pw_ready = sem("pw_ready")
        ypool_out = sem("ypool_out")
        centre_tap = sem("centre_tap")
        taps_done = sem("taps_done")
        silu_done = sem("silu_done")
        og_ready = sem("og_ready")
        ones_set, eps_set, pw_zeroed = sem("ones_set"), sem("eps_set"), sem("pw_zeroed")
        hh_ready, hh_sq = sem("hh_ready"), sem("hh_sq")
        y_raw = sem("y_raw")
        ms_ready, rms_ready, rs_ready = sem("ms_ready"), sem("rms_ready"), sem("rs_ready")
        y_scaled, y_out = sem("y_scaled"), sem("y_out")

        x_rows = {0: [(PAD, meta[:, :]), (64, x_prompt[0, 0:64, :])],
                  1: [(0, x_prompt[0, 64:192, :])],
                  2: [(0, x_prompt[0, 192:256, :]), (112, meta[:, :])]}
        for i in range(3, NT):
            x_rows[i] = [(0, x_sample[0, (i - 3) * P:(i - 2) * P, :])]

        w_blocks = [(0, D_POOL)] + [(D_POOL + w * D_ML + p * PAIR, PAIR) for p in range(2) for w in (0, 3, 1, 2)]

        def tile_cols(i):
            return slice(i * P, (i + 1) * P)

        def row(direction, head):
            return direction * BW + head

        def multiplied(eng, key):
            b, k = plan[key]
            eng.wait_ge(full[b], k)

        def read_out(eng, key):
            b, k = plan[key]
            eng.wait_ge(free[b], k)

        state_key = [k for p in range(2) for k in
                     [("cb1", p, i) for i in range(NT - 1, 0, -1)] + [("cf1", p, i) for i in range(NT)]]
        kw_key = [k for p in range(2) for k in
                  [("kb", p, i) for i in range(NT - 1, 0, -1)] + [("kf", p, i) for i in range(NT)]]
        block_last = [("u", 1, 2)] + [k for p in range(2) for k in
                                      (("qk", p, 0, 2, 2), ("vo", p, NT - 1, 1), ("qk", p, 1, 2, 2), ("vo", p, NT - 1, 0))]

        ORDER = [(1, 0), (1, 1), (0, 0), (0, 1)]


        def slab(n, at=11 * D):
            return arena[:, at + n * D:at + (n + 1) * D]

        y_t = [area("W", Y_W, shift=s * Y_W) for s in range(2)]
        x_t = [area("W", D, shift=2 * Y_W + s * D) for s in range(2)]
        yT_t, x2, t_t, tT_t = ([slab(2 * n + s) for s in range(2)] for n in range(4))
        g2b = arena[:, 8 * D:9 * D]
        wr = arena[:, 9 * D:9 * D + KT * NE].rearrange("p (k e) -> p k e", k=KT)
        L = arena[:, 9 * D + 128:9 * D + 128 + NT * NE].rearrange("p (i e) -> p i e", i=NT)
        AF = arena[0:NE, 9520:9520 + T]
        merge = arena[0:NE, 9520 + T:9520 + T + 2 * CAP_S].rearrange("p (w s) -> p w s", w=2)
        RING = 23 * D
        ring = [arena[:, RING + s * 4096:RING + (s + 1) * 4096].rearrange("p (k n) -> p k n", k=KT) for s in range(6)]
        RANK_S = -(-CAP_S // 8) * 8
        RANKS = 2 * RANK_S + -(-CAP_P // 8) * 8
        vals = arena[0:NE, 48 * D:48 * D + RANKS]
        inds = arena[0:NE, 48 * D + RANKS:48 * D + 2 * RANKS].bitcast(U32)
        ranked = arena[0:NE, 48 * D + 2 * RANKS:48 * D + 2 * RANKS + 2 * SLOTS].rearrange("p (w s) -> p w s", w=2)
        smx = sb("smx", [P, NT])
        idxc = sb("idxc", [P, 2, NE], U32)
        gatec = sb("gatec", [P, 2, NE])
        slot_in = [sem(f"ring{s}_in") for s in range(6)]
        y_in = [sem("y_in0"), sem("y_in1")]
        x3_in = [sem("x3_in0"), sem("x3_in1")]
        x3_clear, g2_in, wr_in = sem("x3_clear"), sem("g2_in"), sem("wr_in")
        x2_ready, x2_sq, t_ready = sem("x2_ready"), sem("x2_sq"), sem("t_ready")
        y_scaled_b = sem("y_scaled_b")
        x2_out = [sem("x2_out0"), sem("x2_out1")]
        t_out = [sem("t_out0"), sem("t_out1")]
        soft_dve, soft_act, aff_ready = sem("soft_dve"), sem("soft_act"), sem("aff_ready")
        topk_step, ranked_ready, idx_ready = sem("topk_step"), sem("ranked_ready"), sem("idx_ready")

        def expert_source(slot, e):
            w = (w_gate, w_up, w_gate, w_up, w_down, w_down)[slot]
            half = (0, 0, 1, 1, 0, 1)[slot]
            return w[0][e, :, half * 512:(half + 1) * 512].rearrange("a (k p) n -> p (a k) n", p=P)

        PADDED = (BT, 0)

        PARTS = ((BT, SPLIT), (SPLIT, NT), (0, BT))
        AF_TILES = ((BT, BT + 4), (BT + 4, SPLIT), (SPLIT, NT), (0, BT))
        RANGES = ((REAL[1][0], SPLIT * P, 0), (SPLIT * P, T, RANK_S), (REAL[0][0], REAL[0][1], 2 * RANK_S))

        def load_y(sp, n):
            i = ORDER_B[n]
            if n >= 2:
                multiplied(sp, ("yT", n - 2, 1))
            sp.dma_start(y_t[n % 2], y_d[i * P:(i + 1) * P, :]).then_inc(y_in[n % 2], 16)

        def load_x3(sp, n):
            i = ORDER_B[n]
            if i in PADDED:
                sp.wait_ge(x3_clear, PADDED.index(i) + 1)
            if n >= 2:
                read_out(sp, ("wo", n - 2, 1))
            for p0, src in x_rows[i]:
                sp.dma_start(x_t[n % 2][p0:p0 + src.shape[0], :], src).then_inc(x3_in[n % 2], 16)

        def x3_count(n):
            return 16 * sum(len(x_rows[ORDER_B[a]]) for a in range(n % 2, n + 1, 2))

        with nc.Block() as block:
            @block.sync
            def _(sp):
                w_view = w_in[0].rearrange("(k p) n -> p k n", p=P)

                def load_w(n):
                    c, w = w_blocks[n]
                    if n >= 2:
                        multiplied(sp, block_last[n - 2])
                    sp.dma_start(Wb[n % 2][:, :, 0:w], w_view[:, :, c:c + w]).then_inc(w_slot_in[n % 2], 16)

                def load_x(i):
                    if i == 0:
                        sp.wait_ge(x_clear, 2)
                    for p0, src in x_rows[i]:
                        sp.dma_start(xin[i][p0:p0 + src.shape[0], :], src).then_inc(x_in[i], 16)

                load_x(ORDER_X[0])
                sp.dma_start(g1b, g1[0:1, :].to_broadcast([P, D])).then_inc(params_in, 16)
                for i in ORDER_X[1:4]:
                    load_x(i)
                sp.wait_ge(zeroed, 2)
                gw = w_in[0][:, 3328:3344].rearrange("(k p) n -> p k n", p=P)
                with nc.allow_non_contiguous_dma(reason="gate columns"):
                    for n, (what, d) in enumerate(((0, 0), (0, 1), (1, 0), (1, 1))):
                        src = gw[:, :, (2 * what + d) * 4:(2 * what + d) * 4 + 4]
                        c = what * NR + d * BW
                        sp.dma_start(Wg[:, :, c:c + 4], src).then_inc(gw_in, 16)
                        sp.dma_start(gb[d * BW:d * BW + 4, what:what + 1],
                                     gate_b[0, 2 * what + d:2 * what + d + 1, :].rearrange("a h -> h a")).then_inc(gb_in, 16)
                sp.dma_start(prow[0:36, :], conv_w[0].rearrange("k (c p) -> (k c) p", p=P)).then_inc(prow_in, 16)
                sp.dma_start(prow[36:48, :], conv_b[0].rearrange("(c p) -> c p", p=P)).then_inc(prow_in, 16)
                for i in ORDER_X[4:]:
                    load_x(i)
                load_w(0)
                load_w(1)
                sp.wait_ge(pw_zeroed, 1)
                for j in range(2):
                    for g in range(2):
                        sp.dma_start(pw[64 * g:64 * g + 64, j, 64 * g:64 * g + 64], pool_w[0, 2 * j + g, :, :]).then_inc(pool_par_in, 16)
                    sp.dma_start(psc[:, j, :], pool_scale[0:1, j * P:(j + 1) * P].to_broadcast([P, P])).then_inc(pool_par_in, 16)
                sp.dma_start(mhg, mh_g[0:1, 0:PAIR].to_broadcast([P, PAIR])).then_inc(mhg_in, 16)
                for j in range(2):
                    if j:
                        sp.wait_ge(mixed_ready, 1)
                    else:
                        read_out(sp, ("par",))
                    for g in range(2):
                        sp.dma_start(rc_t[64 * g:64 * g + 64, :], rcount[2 * j + g:2 * j + g + 1, :].to_broadcast([64, T])).then_inc(params_in, 16)
                for n in range(2, len(w_blocks)):
                    load_w(n)
                    if n == 4:
                        for j in range(2):
                            for g in range(3):
                                read_out(sp, ("po", j, g))
                            sp.dma_start(y_d[:, j * P:(j + 1) * P].rearrange("(i p) n -> p i n", p=P),
                                         ypool[j].rearrange("p (i n) -> p i n", n=P)).then_inc(ypool_out, 16)
                    if n == 6:
                        sp.wait_ge(og_ready, NT)
                        sp.dma_start(mhg, mh_g[0:1, PAIR:D_ML].to_broadcast([P, PAIR])).then_inc(mhg_in, 16)
                        sp.wait_ge(y_scaled, 1)
                        sp.dma_start(y_d[:, D_POOL:D_POOL + PAIR].rearrange("(i p) n -> p i n", p=P),
                                     area("og", NT * PAIR).rearrange("p (i n) -> p i n", i=NT)).then_inc(y_out, 16)
                multiplied(sp, ("vo", 1, NT - 1, 0))
                sp.dma_start(wout, w_out[0].rearrange("(k p) n -> p k n", p=P)).then_inc(wout_in, 16)
                sp.dma_start(g2b, g2[0:1, :].to_broadcast([P, D])).then_inc(g2_in, 16)
                sp.dma_start(wr, w_router[0].rearrange("(k p) e -> p k e", p=P)).then_inc(wr_in, 16)
                sp.wait_ge(ypool_out, 32)
                sp.wait_ge(y_out, 16)
                for n in range(2):
                    load_y(sp, n)
                    load_x3(sp, n)

            @block.gpsimd
            def _(pool):
                st = Steps(pool, pool_step)
                st.do(pool.memset(ident[:, :], 0.0))
                st.do(pool.memset(masks[:, :, :, :], 0.0))
                st.settle()
                pool.affine_select(out=ident[:, :], in_=ident[:, :], compare_op=ALU.not_equal, fill=1.0, base=0,
                                   pattern=[[-1, P]], channel_multiplier=1).then_inc(ident_done, 1)
                for b in range(2):
                    for q, d in enumerate((1, 0)):
                        sgn = 1 if d == 0 else -1
                        st.do(pool.affine_select(out=masks[:, b, q, :], in_=masks[:, b, q, :], compare_op=ALU.is_ge,
                                                 fill=NEG, base=0, pattern=[[sgn, P]], channel_multiplier=-sgn))
                st.settle()
                half = BOUND % P
                st.do(pool.memset(masks[0:half, 1, :, half:P], NEG))
                st.settle()
                pool.memset(masks[half:P, 1, :, 0:half], NEG).then_inc(masks_done, 1)

                pool.wait_ge(masks_done, 1)
                pool.wait_ge(pool_par_in, 96)
                pool.tensor_tensor(pw[:, :, :], pw[:, :, :], psc[:, :, :], ALU.mult).then_inc(pw_ready, 1)

                def shifted(out, a, lo, hi, d0, d1, parts=slice(0, P)):
                    st.do(pool.tensor_tensor(out[parts, lo:hi], a[parts, lo + d0:hi + d0], a[parts, lo + d1:hi + d1], ALU.add))
                    st.settle()

                lo_h, hi_h = slice(0, 64), slice(64, P)
                body = slice(8, 8 + T)
                for j in range(2):
                    read_out(pool, ("u", j, 2))
                    shifted(PA, U, 1, 1424, -1, 0)
                    shifted(PB, PA, 2, 1423, -1, 1)
                    dst = mix0 if j == 0 else PA[:, body]
                    if j == 1:
                        shifted(PA, PB, 4, 1421, -2, 2)
                        shifted(PB, PA, 8, 1416, -4, 4, hi_h)
                    pool.wait_ge(params_in, 16 + 32 * (j + 1))
                    st.do(pool.tensor_tensor(dst[lo_h, :], PA[lo_h, body], rc_t[lo_h, :], ALU.mult))
                    st.settle()
                    st.do(pool.tensor_tensor(dst[hi_h, :], PB[hi_h, body], rc_t[hi_h, :], ALU.mult))
                    st.settle()
                    pool.tensor_tensor(dst, dst, U[:, body], ALU.subtract).then_inc(mixed_ready, 1)

                for p in range(2):
                    for i in range(NT):
                        read_out(pool, ("vo", p, i, 1))
                        if i == 0:
                            pool.wait_ge(mhg_in, 16 * (p + 1))
                        pool.tensor_tensor(og[:, i, :, :], og[:, i, :, :],
                                           mhg.rearrange("p (h d) -> p h d", h=2), ALU.mult).then_inc(og_ready, 1)
                    for i in range(NT):
                        pool.wait_ge(hh_ready, p * NT + i + 1)
                        pool.wait_ge(og_ready, p * NT + i + 1)
                        pool.tensor_tensor(og[:, i, :, :], og[:, i, :, :], hh[:, i % 2, :, :], ALU.mult).then_inc(y_raw, 1)
                    pool.wait_ge(y_raw, (p + 1) * NT)
                    if p == 1:
                        break
                    pool.wait_ge(rs_ready, 1)
                    ogf = area("og", NT * PAIR).rearrange("p (n d) -> p n d", d=HD)
                    pool.tensor_tensor(ogf, ogf, ss_h[:, :].unsqueeze(2).to_broadcast([P, 2 * NT, HD]), ALU.mult).then_inc(y_scaled, 1)

            @block.scalar
            def _(act):
                st = Steps(act, act_step)

                def evac(key, out, src, func=ACT.Copy, **kw_):
                    b, k = plan[key]
                    act.wait_ge(full[b], k)
                    return act.activation(out, src(ps[b]), func, **kw_).then_inc(free[b], 1)

                def move_xT(i):
                    evac(("x", i, 0), hT[:, 0:4, tile_cols(ORDER_X[i])], lambda b: b[:, :].rearrange("p (k t) -> p k t", k=4))

                for i in range(NT):
                    tile = ORDER_X[i]
                    act.wait_ge(x_in[tile], 16 * len(x_rows[tile]))
                    st.do(act.activation(area("Pm", D), xin[tile], ACT.Square, accum_out=small[:, i:i + 1]))
                    if i == 0:
                        act.wait_ge(eps_set, 1)
                    st.settle()
                    act.activation(small[:, 32 + i:33 + i], small[:, i:i + 1], ACT.Sqrt, scale=1.0 / D, bias=small[:, 94:95]).then_inc(sq_done, 1)
                    if i:
                        move_xT(i - 1)
                move_xT(NT - 1)
                evac(("par",), par[:, 0:48], lambda b: b[:, 0:48])
                for i in range(NT):
                    evac(("g", i), gtok[:, i, :], lambda b: b[:, 0:2 * NR])
                act.wait_ge(rows_dve, 1)
                st.do(act.activation(R[2], R[1], ACT.Abs))
                st.settle()
                st.do(act.activation(R[2], R[2], ACT.Exp, scale=-1.0))
                st.settle()
                act.activation(R[2], R[2], ACT.Ln, bias=1.0).then_inc(rows_act, 1)
                for j in range(2):
                    if j:
                        act.wait_ge(mixed_ready, 1)
                    for c, (lo, hi) in enumerate(CHUNKS):
                        b, k = plan[("u", j, c)]
                        act.wait_ge(full[b], k)
                        if j == 0 and c == 0:
                            act.wait_ge(zeroed, 3)
                        act.activation(U[:, 8 + lo:8 + hi], ps[b][:, 0:hi - lo], ACT.Copy).then_inc(free[b], 1)

                def rows_out(out, src, func, **kw_):
                    st.do(act.activation(out[0:BW, :], src[0:BW, :], func, **kw_))
                    st.do(act.activation(out[BW:NR, :], src[BW:NR, ::-1], func, **kw_))

                def gate_rows_first():
                    act.wait_ge(rows_dve, 2)
                    for lo_p, hi_p, rev in ((0, BW, slice(None)), (BW, NR, slice(None, None, -1))):
                        st.do(act.activation(R[1][lo_p:hi_p, :], R[2][lo_p:hi_p, rev], ACT.Exp, bias=small[lo_p:hi_p, 95:96]))
                    rows_out(S1[:, :], S0[:, :], ACT.Exp)

                def gate_rows_rest():
                    st.settle()
                    rows_out(R[2], R[6], ACT.Exp)
                    rows_out(R[3], R[5], ACT.Exp, scale=-1.0)
                    rows_out(negM, R[4], ACT.Copy, scale=-1.0)
                    st.settle()
                    rows_out(R[5], R[0], ACT.Copy, bias=LN_SCALE)
                    st.settle()
                    act.sem_inc(rows_ready, 1)

                def conv_centre(p, w, j):
                    n = (p * 2 + w) * 3 + j
                    if n:
                        act.wait_ge(taps_done, n)
                    if n == 3:
                        act.wait_ge(ypool_out, 32)
                    for c, (lo, hi) in enumerate(CHUNKS):
                        b, k = plan[("qk", p, w, j, c)]
                        act.wait_ge(full[b], k)
                        if n == 0 and c == 0:
                            act.wait_ge(zeroed, 4)
                        act.activation(Z[:, 1 + lo:1 + hi], ps[b][:, 0:hi - lo], ACT.Copy).then_inc(free[b], 1)
                    act.wait_ge(free[b], k)
                    ct = w * 6 + p * 3 + j
                    act.activation(qkT[w][:, j, :], Z[:, 1:1 + T], ACT.Identity, scale=par[:, 12 + ct:13 + ct],
                                   bias=par[:, 36 + ct:37 + ct]).then_inc(centre_tap, 1)

                def silu(p, w, j):
                    n = (p * 2 + w) * 3 + j
                    act.wait_ge(taps_done, n + 1)
                    if w == 0 and j == 1:
                        if p == 0:
                            act.wait_ge(zeroed, 5)
                        st.do(act.activation(q1h[64:P, :], qT[64:P, 1, :], ACT.Silu))
                        st.do(act.activation(qT[0:64, 1, :], qT[0:64, 1, :], ACT.Silu))
                        act.memzero(qT[64:P, 1, :]).then_inc(silu_done, 1)
                    else:
                        act.activation(qkT[w][:, j, :], qkT[w][:, j, :], ACT.Silu).then_inc(silu_done, 1)

                def weigh_keys(key, p, i, d, n):
                    b, k = plan[key]
                    act.wait_ge(full[b], k)
                    if n >= 2:
                        multiplied(act, state_key[n - 2])
                    for h in range(2):
                        r = row(d, 2 * p + h)
                        last = act.activation(kw[:, n % 2, h, :], ps[b][:, h * HD:(h + 1) * HD], ACT.Copy, scale=cols[:, i, 1, r:r + 1])
                    last.then_inc(free[b], 1)

                def decays(p, i, n):
                    act.wait_ge(full[3], n + 1)
                    if n:
                        read_out(act, ("S", (n - 1) // NT, (n - 1) % NT))
                    for q, (d, h) in enumerate(ORDER):
                        r = row(d, 2 * p + h)
                        last = act.activation(E[:, q * P:(q + 1) * P], ps[3][:, q * P:(q + 1) * P], ACT.Exp,
                                              bias=cols[:, i, 3, r:r + 1])
                    last.then_inc(free[3], 1)

                def square_hh(p, i):
                    act.wait_ge(hh_ready, p * NT + i + 1)
                    if p and i == 0:
                        act.wait_ge(y_scaled, 1)
                    for h in range(2):
                        if p + i + h:
                            act.wait_ge(hh_sq, 2 * (p * NT + i) + h)
                        act.activation(junk_h, hh[:, i % 2, h, :], ACT.Square, accum_out=ss_h[:, 2 * i + h:2 * i + h + 1]).then_inc(hh_sq, 1)

                for p in range(2):
                    for w in range(2):
                        for j in range(3):
                            conv_centre(p, w, j)
                            silu(p, w, j)
                            if (p, w, j) == (0, 0, 0):
                                gate_rows_first()
                            if (p, w, j) == (0, 0, 1):
                                gate_rows_rest()
                        if w == 0:
                            if p == 1:
                                act.wait_ge(y_out, 16)
                            for i in range(NT):
                                evac(("vo", p, i, 1), og[:, i, :, :], lambda b: b[:, 0:PAIR].rearrange("p (h d) -> p h d", h=2), ACT.Sigmoid)
                        if p == 0 and w == 0:
                            for i in range(NT):
                                evac(("rc", i), cols[:, i, :, :], lambda b: b[:, 0:4 * NR].rearrange("p (a n) -> p a n", a=4))
                            evac(("sp",), spc[:, :, :], lambda b: b[:, 0:12 * NT].rearrange("p (a n) -> p a n", a=12))
                            act.wait_ge(mixed_ready, 2)
                            for n in range(6):
                                lo = 512 * (n % 3)
                                wd = min(512, T - lo)
                                evac(("po", n // 3, n % 3), ypool[n // 3][:, lo:lo + wd], lambda b, wd=wd: b[:, 0:wd])
                    if p == 0:
                        read_out(act, ("sp",))
                    for i in range(NT):
                        b, k = plan[("vo", p, i, 0)]
                        if i == 0:
                            act.wait_ge(ones_set, 1)
                        evac(("vo", p, i, 0), v[:, i, :, 0:HD], lambda b: b[:, 0:PAIR].rearrange("p (h d) -> p h d", h=2))
                    n = p * (2 * NT - 1)
                    for i in range(NT - 1, 0, -1):
                        weigh_keys(("kb", p, i), p, i, 1, n)
                        n += 1
                    decays(p, 0, p * NT)
                    for i in range(NT):
                        weigh_keys(("kf", p, i), p, i, 0, n)
                        n += 1
                        m = p * NT + i
                        for half in range(2):
                            act.wait_ge(full[4 + half], m + 1)
                            if m and half == 0:
                                act.wait_ge(free[7], m)
                            for hd in range(2):
                                q = 2 * half + hd
                                r = row(ORDER[q][0], 2 * p + hd)
                                last = act.activation(inter[:, q, :], ps[4 + half][:, hd * VW:(hd + 1) * VW], ACT.Copy,
                                                      scale=cols[:, i, 0, r:r + 1])
                            last.then_inc(free[4 + half], 1)
                        if i + 1 < NT:
                            decays(p, i + 1, m + 1)
                        if i:
                            square_hh(p, i - 1)
                    square_hh(p, NT - 1)
                    act.wait_ge(ms_ready, p + 1)
                    act.activation(ss_h[:, :], ss_h[:, :], ACT.Sqrt).then_inc(rms_ready, 1)

            @block.vector
            def _(dve):
                st = Steps(dve, dve_step)
                dve.memset(xin[0][0:64, :], 0.0).then_inc(x_clear, 1)
                dve.memset(xin[BT][64:P, :], 0.0).then_inc(x_clear, 1)
                dve.memset(small[:, 94:95], EPS).then_inc(eps_set, 1)
                dve.memset(Wg[:, :, :], 0.0).then_inc(zeroed, 1)
                dve.memset(gb[:, :], 0.0).then_inc(zeroed, 1)
                st.do(dve.memset(q1h[0:64, :], 0.0))
                dve.memset(pw[:, :, :], 0.0).then_inc(pw_zeroed, 1)
                st.do(dve.memset(small[:, 95:96], LN_SCALE))
                dve.wait_ge(ident_done, 1)
                st.do(dve.tensor_copy(ident_b[:, :], ident[:, :]))
                def move_xT(i):
                    multiplied(dve, ("x", i, 1))
                    b = plan[("x", i, 1)][0]
                    dve.tensor_copy(hT[:, 4:8, tile_cols(ORDER_X[i])], ps[b][:, :].rearrange("p (k t) -> p k t", k=4)).then_inc(free[b], 1)

                for i in range(NT):
                    dve.wait_ge(sq_done, i + 1)
                    st.do(dve.reciprocal(small[:, 48 + i:49 + i], small[:, 32 + i:33 + i]))
                    if i == 0:
                        dve.wait_ge(params_in, 16)
                    if i >= 2:
                        multiplied(dve, ("x", i - 2, 1))
                    st.settle()
                    dve.scalar_tensor_tensor(xn[i % 2], xin[ORDER_X[i]], small[:, 48 + i:49 + i], g1b, ALU.mult, ALU.mult).then_inc(xn_done, 1)
                    if i:
                        move_xT(i - 1)
                move_xT(NT - 1)
                st.do(dve.memset(R[6], 1.0))
                st.settle()
                st.do(dve.memset(R[6][:, 0:T:P], 0.0))
                st.do(dve.memset(R[6][0:4, BOUND:BOUND + 1], 0.0))
                st.do(dve.memset(R[6][BW:NR, T - BOUND:T - BOUND + 1], 0.0))
                for i in range(NT):
                    b, k = plan[("gt", i)]
                    dve.wait_ge(full[b], k)
                    src = ps[b][0:NR, 0:2 * P].rearrange("p (r t) -> p r t", r=2)
                    st.do(dve.tensor_copy(R01[0:BW, :, tile_cols(i)], src[0:BW, :, :]))
                    dve.tensor_copy(R01[BW:NR, :, tile_cols(NT - 1 - i)], src[BW:NR, :, ::-1]).then_inc(free[b], 1)
                dve.wait_ge(free[b], k)
                dve.memset(U[:, 0:8], 0.0)
                dve.memset(U[:, 8 + T:1424], 0.0).then_inc(zeroed, 1)
                dve.memset(Z[:, 0:1], 0.0)
                dve.memset(Z[:, 1 + T:2 + T], 0.0).then_inc(zeroed, 1)
                dve.sem_inc(zeroed, 1)
                dve.wait_ge(gb_in, 64)
                st.do(dve.tensor_scalar(R[0], R[0], gb[:, 0:1], None, ALU.add))
                st.do(dve.tensor_scalar(R[1], R[1], gb[:, 1:2], None, ALU.add))
                st.settle()
                dve.sem_inc(rows_dve, 1)
                dve.wait_ge(rows_act, 1)
                st.do(dve.scalar_tensor_tensor(R[1], R[1], 0.0, R[2], ALU.min, ALU.subtract))
                st.settle()
                for lo, _ in REAL:
                    for ap, c0 in ((slice(0, 4), lo - PAD), (slice(BW, NR), T - lo)):
                        st.do(dve.memset(R[0][ap, c0:c0 + PAD], NEG))
                        st.do(dve.memset(R[1][ap, c0:c0 + PAD], 0.0))
                st.settle()
                st.do(dve.tensor_tensor_scan(R[3], R[6], R[1], 0.0, ALU.mult, ALU.add))
                st.settle()
                st.do(dve.tensor_tensor(R[0], R[0], R[3], ALU.subtract))
                st.do(dve.memset(R[6], 0.0))
                st.settle()
                st.do(dve.tensor_copy(R[2], R[0]))
                st.do(dve.tensor_copy(R[6][:, P:T:P], R[3][:, P - 1:T - P:P]))
                st.settle()
                for ap, c0 in ((slice(0, 4), BOUND), (slice(BW, NR), T - BOUND)):
                    st.do(dve.memset(R[6][ap, c0:c0 + 1], NEG))
                    st.do(dve.tensor_scalar(R[2][ap, c0:c0 + 1], R[0][ap, c0:c0 + 1], 0.0, None, ALU.max))
                st.settle()
                st.do(dve.tensor_tensor_scan(R[4], R[6], R[2], 0.0, ALU.add, ALU.max))
                st.settle()
                st.do(dve.tensor_tensor(R[5], R[3], R[4], ALU.add))
                st.do(dve.memset(R[6][:, 0:P], 0.0))
                st.settle()

                def tiles(ap):
                    return ap.rearrange("p (i t) -> p i t", t=P)

                st.do(dve.tensor_copy(tiles(R[6])[:, 1:NT, :], R[5][:, P - 1:T - P:P].unsqueeze(2).to_broadcast([NR, NT - 1, P])))
                st.settle()
                st.do(dve.tensor_tensor(R[2], R[6], R[4], ALU.subtract))
                st.do(dve.tensor_tensor(S0[:, :], R[6][:, 0:T:P], R[4][:, P - 1:T:P], ALU.subtract))
                st.settle()
                half = BOUND % P
                for ap, c0, s in ((slice(0, 4), BOUND, BT), (slice(BW, NR), T - BOUND, NT - 1 - BT)):
                    st.do(dve.memset(R[2][ap, c0:c0 + P - half], NEG))
                    st.do(dve.memset(S0[ap, s:s + 1], NEG))
                st.do(dve.tensor_tensor(tiles(R[6]), tiles(R[0]), R[4][:, P - 1:T:P].unsqueeze(2).to_broadcast([NR, NT, P]), ALU.subtract))
                st.settle()
                for ap, c0 in ((slice(0, 4), BOUND), (slice(BW, NR), T - BOUND)):
                    st.do(dve.memset(R[6][ap, c0 - half:c0], NEG))
                st.settle()
                dve.sem_inc(rows_dve, 1)

                def outer_taps(p, w, j):
                    n = (p * 2 + w) * 3 + j
                    ct = w * 6 + p * 3 + j
                    dve.wait_ge(centre_tap, n + 1)
                    o = qkT[w][:, j, :]
                    st.do(dve.scalar_tensor_tensor(o, Z[:, 0:T], par[:, ct:ct + 1], o, ALU.mult, ALU.add))
                    st.settle()
                    dve.scalar_tensor_tensor(o, Z[:, 2:2 + T], par[:, 24 + ct:25 + ct], o, ALU.mult, ALU.add).then_inc(taps_done, 1)

                def update_state(new, old, k0, k1, p, d, i):
                    for j in range(3):
                        b, k = plan[k0 if j < 2 else k1]
                        if j != 1:
                            dve.wait_ge(full[b], k)
                        a = (p * 2 + d) * 3 + j
                        c = (j % 2) * VW
                        last = dve.scalar_tensor_tensor(new[:, j, :], old[:, j, :], spc[:, a, i:i + 1], ps[b][:, c:c + VW], ALU.mult, ALU.add)
                        if j == 0:
                            st.do(last)
                        else:
                            last.then_inc(free[b], 1)
                    dve.wait_ge(free[b], k)

                for p in range(2):
                    for w in range(2):
                        for j in range(3):
                            outer_taps(p, w, j)
                    if p == 0:
                        b, k = plan[("rc", NT - 1)]
                        dve.wait_ge(full[b], k)
                        dve.memset(v[:, :, :, HD:VW], 1.0).then_inc(ones_set, 1)
                        st.do(dve.memset(Cb[:, NT - 1, :, :], 0.0))
                        b, k = plan[("sp",)]
                        dve.wait_ge(free[b], k)
                    if p == 1:
                        multiplied(dve, ("vo", 1, NT - 1, 0))
                        dve.memset(x_t[0][64:P, :], 0.0).then_inc(x3_clear, 1)
                    st.do(dve.memset(Cf[:, :, :], 0.0))
                    st.settle()
                    for i in range(NT - 1, 0, -1):
                        update_state(Cb[:, i - 1, :, :], Cb[:, i, :, :], ("cb0", p, i), ("cb1", p, i), p, 1, i)
                    for i in range(NT):
                        m = p * NT + i
                        dve.wait_ge(free[3], m + 1)
                        b, k = plan[("S", p, i)]
                        dve.wait_ge(full[b], k)
                        if m:
                            dve.wait_ge(full[7], m)
                        S = ps[b][:, 0:2 * P].rearrange("p (h t) -> p h t", h=2).unsqueeze(1).to_broadcast([P, 2, 2, P])
                        e4 = E.rearrange("p (d h t) -> p d h t", d=2, h=2)
                        dve.tensor_tensor(Pm.rearrange("p (d h t) -> p d h t", d=2, h=2), S, e4, ALU.mult).then_inc(free[b], 1)
                        update_state(Cf, Cf, ("cf0", p, i), ("cf1", p, i), p, 0, i)
                        for half in range(2):
                            dve.wait_ge(free[4 + half], m + 1)
                            dve.wait_ge(full[6 + half], m + 1)
                            q = slice(2 * half, 2 * half + 2)
                            dve.tensor_tensor(num[:, q, :], ps[6 + half][:, 0:2 * VW].rearrange("p (q d) -> p q d", q=2),
                                              inter[:, q, :], ALU.add).then_inc(free[6 + half], 1)
                        dve.wait_ge(free[7], m + 1)
                        den = num[:, :, HD]
                        st.do(dve.scalar_tensor_tensor(small[:, 0:4], den, -1.0, den, ALU.mult, ALU.max))
                        st.settle()
                        for half, d in ((0, 1), (1, 0)):
                            r = row(d, 2 * p)
                            st.do(dve.tensor_tensor(small[:, 4 + 2 * half:6 + 2 * half], small[:, 2 * half:2 * half + 2], cols[:, i, 2, r:r + 2], ALU.max))
                        st.settle()
                        st.do(dve.reciprocal(small[:, 8:12], small[:, 4:8]))
                        if m >= 2:
                            dve.wait_ge(hh_sq, 2 * (m - 1))
                            dve.wait_ge(y_raw, m - 1)
                        st.settle()
                        for h in range(2):
                            st.do(dve.tensor_scalar(hh[:, i % 2, h, :], num[:, h, 0:HD], small[:, 8 + h:9 + h], None, ALU.mult))
                        st.settle()
                        for h in range(2):
                            st.do(dve.scalar_tensor_tensor(hh[:, i % 2, h, :], num[:, 2 + h, 0:HD], small[:, 10 + h:11 + h],
                                                           hh[:, i % 2, h, :], ALU.mult, ALU.add))
                        st.settle()
                        dve.sem_inc(hh_ready, 1)
                    dve.wait_ge(hh_sq, 2 * (p + 1) * NT)
                    dve.tensor_scalar(ss_h[:, :], ss_h[:, :], 1.0 / HD, EPS, ALU.mult, ALU.add).then_inc(ms_ready, 1)
                    dve.wait_ge(rms_ready, p + 1)
                    dve.reciprocal(ss_h[:, :], ss_h[:, :]).then_inc(rs_ready, 1)

            @block.tensor
            def _(pe):
                def bank(key):
                    b, k = plan[key]
                    if k > 1:
                        pe.wait_ge(free[b], k - 1)
                    return b

                pe.wait_ge(ident_done, 1)
                for i in range(NT):
                    pe.wait_ge(xn_done, i + 1)
                    for h in range(2):
                        b = bank(("x", i, h))
                        for k in range(4):
                            c = (4 * h + k) * P
                            last = pe.transpose(ps[b][:, k * P:(k + 1) * P], xn[i % 2][:, c:c + P], ident[:, :])
                        last.then_inc(full[b], 1)
                pe.wait_ge(prow_in, 32)
                b = bank(("par",))
                pe.transpose(ps[b][:, 0:48], prow[0:48, :], ident[0:48, 0:48]).then_inc(full[b], 1)
                pe.wait_ge(gw_in, 64)
                for h in range(2):
                    read_out(pe, ("x", NT - 1, h))
                for i in range(NT + 1):
                    if i < NT:
                        b = bank(("g", i))
                        for k in range(KT):
                            last = pe.matmul(ps[b][:, 0:2 * NR], hT[:, k, tile_cols(i)], Wg[:, k, :], start=k == 0, stop=k == KT - 1)
                        last.then_inc(full[b], 1)
                    if i:
                        bg, kg = plan[("g", i - 1)]
                        pe.wait_ge(free[bg], kg)
                        b = bank(("gt", i - 1))
                        for r in range(2):
                            last = pe.transpose(ps[b][0:NR, r * P:(r + 1) * P], gtok[:, i - 1, r * NR:(r + 1) * NR], ident[:, :])
                        last.then_inc(full[b], 1)
                pe.wait_ge(w_slot_in[0], 16)
                for j in range(2):
                    for c, (lo, hi) in enumerate(CHUNKS):
                        b = bank(("u", j, c))
                        for k in range(KT):
                            last = pe.matmul(ps[b][:, 0:hi - lo], Wb[0][:, k, j * P:(j + 1) * P], hT[:, k, lo:hi], start=k == 0, stop=k == KT - 1)
                        last.then_inc(full[b], 1)

                def state_products(k0, k1, p, i, n, d):
                    read_out(pe, kw_key[n])
                    b0 = bank(k0)
                    s = n % 2
                    kwf = kw[:, s, :, :].rearrange("p h d -> p (h d)")
                    pe.matmul(ps[b0][:, 0:VW], kwf[:, 0:P], v[:, i, 0, :], start=True, stop=True)
                    pe.matmul(ps[b0][0:64, VW:2 * VW], kwf[:, P:HD], v[:, i, 0, :], start=True, stop=True)
                    pe.matmul(ps[b0][64:P, VW:2 * VW], kwf[:, HD:2 * P], v[:, i, 1, :], start=True, stop=True).then_inc(full[b0], 1)
                    b1 = bank(k1)
                    pe.matmul(ps[b1][:, 0:VW], kwf[:, 2 * P:3 * P], v[:, i, 1, :], start=True, stop=True).then_inc(full[b1], 1)

                def decay_exponents(p, i, n):
                    if n:
                        pe.wait_ge(free[3], n)
                    pe.matmul(ps[3][:, :], ident_b[:, :], masks[:, 1 if i == BT else 0, :, :].unsqueeze(2).to_broadcast([P, 2, 2, P]),
                              start=True, stop=False)
                    for q, (d, h) in enumerate(ORDER):
                        r = row(d, 2 * p + h)
                        last = pe.matmul(ps[3][:, q * P:(q + 1) * P], ident[0:NR, r:r + 1].to_broadcast([NR, P]),
                                         negM[0:NR, tile_cols(i)], start=False, stop=q == 3)
                    last.then_inc(full[3], 1)

                def queries(h, i):
                    c = tile_cols(i)
                    return ((qT[:, 0, c], 0), (qT[:, 1, c], 1)) if h == 0 else ((q1h[:, c], 1), (qT[:, 2, c], 2))

                def transpose_keys(key, i):
                    b = bank(key)
                    for j in range(3):
                        last = pe.transpose(ps[b][:, j * P:(j + 1) * P], kT[:, j, tile_cols(i)], ident[:, :])
                    last.then_inc(full[b], 1)

                def tokens_by_block(p, w, nb):
                    pe.wait_ge(w_slot_in[nb % 2], 16 * (nb // 2 + 1))
                    for i in range(NT):
                        b = bank(("vo", p, i, w))
                        for k in range(KT):
                            last = pe.matmul(ps[b][:, 0:PAIR], hT[:, k, tile_cols(i)], Wb[nb % 2][:, k, :], start=k == 0, stop=k == KT - 1)
                        last.then_inc(full[b], 1)

                pe.wait_ge(masks_done, 1)
                for p in range(2):
                    for w in range(2):
                        nb = 1 + 4 * p + 2 * w
                        pe.wait_ge(w_slot_in[nb % 2], 16 * (nb // 2 + 1))
                        for j in range(3):
                            for c, (lo, hi) in enumerate(CHUNKS):
                                b = bank(("qk", p, w, j, c))
                                for k in range(KT):
                                    last = pe.matmul(ps[b][:, 0:hi - lo], Wb[nb % 2][:, k, j * P:(j + 1) * P], hT[:, k, lo:hi],
                                                     start=k == 0, stop=k == KT - 1)
                                last.then_inc(full[b], 1)
                        if w == 0:
                            tokens_by_block(p, 1, 2 + 4 * p)
                        if p == 0 and w == 0:
                            pe.wait_ge(rows_ready, 1)
                            for i in range(NT):
                                b = bank(("rc", i))
                                for n, rr in enumerate((R[1], R[2], R[3], R[5])):
                                    last = pe.transpose(ps[b][:, n * NR:(n + 1) * NR], rr[:, tile_cols(i)], ident[0:NR, 0:NR])
                                last.then_inc(full[b], 1)
                            b = bank(("sp",))
                            for pp in range(2):
                                for d in range(2):
                                    for j in range(3):
                                        a = ((pp * 2 + d) * 3 + j) * NT
                                        for h in ((0,), (0, 1), (1,))[j]:
                                            parts = slice(0, P) if j != 1 else slice(64 * h, 64 * h + 64)
                                            n = P if j != 1 else 64
                                            r = row(d, 2 * pp + h)
                                            last = pe.matmul(ps[b][parts, a:a + NT], ident[0:NR, r:r + 1].to_broadcast([NR, n]),
                                                             S1[:, :], start=True, stop=True)
                            last.then_inc(full[b], 1)
                            pe.wait_ge(pw_ready, 1)
                            for j in range(2):
                                pe.wait_ge(mixed_ready, j + 1)
                                src = mix0 if j == 0 else PA[:, 8:8 + T]
                                for g in range(3):
                                    b = bank(("po", j, g))
                                    for a in range(4 * g, min(4 * g + 4, NT)):
                                        c = (a - 4 * g) * P
                                        last = pe.matmul(ps[b][:, c:c + P], src[:, tile_cols(a)], pw[:, j, :], start=True, stop=True)
                                    last.then_inc(full[b], 1)
                    tokens_by_block(p, 0, 4 + 4 * p)
                    n = p * (2 * NT - 1)
                    pe.wait_ge(silu_done, 6 * (p + 1))
                    b, k = plan[("vo", p, NT - 1, 0)]
                    pe.wait_ge(free[b], k)
                    transpose_keys(("kb", p, NT - 1), NT - 1)
                    for i in range(NT - 1, 0, -1):
                        if i > 1:
                            transpose_keys(("kb", p, i - 1), i - 1)
                        state_products(("cb0", p, i), ("cb1", p, i), p, i, n, 1)
                        n += 1
                    decay_exponents(p, 0, p * NT)
                    for i in range(NT):
                        m = p * NT + i
                        b = bank(("S", p, i))
                        for h in range(2):
                            for a, (q, j) in enumerate(queries(h, i)):
                                last = pe.matmul(ps[b][:, h * P:(h + 1) * P], kT[:, j, tile_cols(i)], q,
                                                 start=a == 0, stop=a == 1)
                        last.then_inc(full[b], 1)
                        transpose_keys(("kf", p, i), i)
                        for half, d in ((0, 1), (1, 0)):
                            if m:
                                pe.wait_ge(free[4 + half], m)
                            read_out(pe, ("cf1", p, i - 1) if d == 0 and i else ("cb1", p, 1))
                            for h in range(2):
                                for a, (q, j) in enumerate(queries(h, i)):
                                    C = Cb[:, i, j, :] if d == 1 else Cf[:, j, :]
                                    last = pe.matmul(ps[4 + half][:, h * VW:(h + 1) * VW], q, C,
                                                     start=a == 0, stop=a == 1)
                            last.then_inc(full[4 + half], 1)
                        if i + 1 < NT:
                            decay_exponents(p, i + 1, m + 1)
                        state_products(("cf0", p, i), ("cf1", p, i), p, i, n, 0)
                        n += 1
                        read_out(pe, ("S", p, i))
                        for half in range(2):
                            if m:
                                pe.wait_ge(free[6 + half], m)
                            for h in range(2):
                                q = 2 * half + h
                                last = pe.matmul(ps[6 + half][:, h * VW:(h + 1) * VW], Pm[:, q * P:(q + 1) * P], v[:, i, h, :],
                                                 start=True, stop=True)
                            last.then_inc(full[6 + half], 1)

        with nc.Block() as block:
            @block.sync
            def _(sp):
                def load_expert(s):
                    sp.dma_start(ring[s], expert_source(s, slice(0, 1))).then_inc(slot_in[s], 16)

                for n in range(NT):
                    if n + 2 < NT:
                        load_y(sp, n + 2)
                        load_x3(sp, n + 2)
                    if n in (0, 1, 2):
                        load_expert((1, 4, 5)[n])
                    if n == NT - BT - 1:
                        multiplied(sp, ("yT", n, 1))
                        load_expert(0)
                    i = ORDER_B[n]
                    sp.wait_ge(x2_ready, 2 * (n + 1))
                    sp.dma_start(acc_d[i * P:(i + 1) * P, :], x2[n % 2]).then_inc(x2_out[n % 2], 16)
                    sp.wait_ge(t_ready, n + 1)
                    sp.dma_start(t_d[i * P:(i + 1) * P, :], t_t[n % 2]).then_inc(t_out[n % 2], 16)
                for h in range(2):
                    read_out(sp, ("wo", NT - 1, h))
                load_expert(2)
                load_expert(3)
                for s in range(2):
                    n = 16 * len(range(s, NT, 2))
                    sp.wait_ge(x2_out[s], n)
                    sp.wait_ge(t_out[s], n)

            @block.gpsimd
            def _(pool):
                for i in ORDER_B:
                    pool.tensor_tensor(og[:, i, :, :], og[:, i, :, :], ss_h[:, 2 * i:2 * i + 2].unsqueeze(2).to_broadcast([P, 2, HD]),
                                       ALU.mult).then_inc(y_scaled_b, 1)

            @block.scalar
            def _(act):
                st = Steps(act, sem("act_step_b"))

                def move(key, out, parts=P, w=512):
                    multiplied(act, key)
                    act.activation(out, ps[plan[key][0]][0:parts, 0:w], ACT.Copy).then_inc(free[plan[key][0]], 1)

                def halves(name, n, slots):
                    for h in range(2):
                        move((name, n, h), slots[n % 2][:, 512 * h:512 * h + 512])

                def exponentials(part):
                    lo, hi = PARTS[part]
                    act.wait_ge(soft_dve, part + 1)
                    act.activation(L[:, lo:hi, :], L[:, lo:hi, :], ACT.Exp).then_inc(soft_act, 1)

                def affinities(g):
                    lo, hi = AF_TILES[g]
                    move(("af", g), AF[:, lo * P:hi * P], NE, (hi - lo) * P)

                halves("yT", 0, yT_t)
                for n in range(NT + 1):
                    if n:
                        halves("tT", n - 1, tT_t)
                    if n + 1 < NT:
                        halves("yT", n + 1, yT_t)
                    if n:
                        move(("lg", n - 1), L[:, ORDER_B[n - 1], :], P, NE)
                    if n == STEP_A:
                        exponentials(0)
                    if n == STEP_B:
                        exponentials(1)
                    if n < NT:
                        act.wait_ge(x2_ready, 2 * (n + 1))
                        if n:
                            st.settle()
                        st.do(act.activation(junk_b, x2[n % 2], ACT.Square, accum_out=small[:, n:n + 1]))
                        st.settle()
                        act.activation(small[:, 32 + n:33 + n], small[:, n:n + 1], ACT.Sqrt, scale=1.0 / D, bias=small[:, 94:95]).then_inc(x2_sq, 1)
                    if n == STEP_A:
                        affinities(0)
                        affinities(1)
                    if n == STEP_B:
                        affinities(2)
                exponentials(2)
                affinities(3)

            @block.vector
            def _(dve):
                st = Steps(dve, topk_step)

                def add(n, h):
                    multiplied(dve, ("wo", n, h))
                    b = plan[("wo", n, h)][0]
                    c = slice(512 * h, 512 * h + 512)
                    dve.tensor_tensor(x2[n % 2][:, c], ps[b][:, :], x_t[n % 2][:, c], ALU.add).then_inc(free[b], 1)
                    read_out(dve, ("wo", n, h))
                    dve.sem_inc(x2_ready, 1)

                def norm(n):
                    dve.wait_ge(x2_sq, n + 1)
                    st.do(dve.reciprocal(small[:, 48 + n:49 + n], small[:, 32 + n:33 + n]))
                    if n == 0:
                        dve.wait_ge(g2_in, 16)
                    st.settle()
                    dve.scalar_tensor_tensor(t_t[n % 2], x2[n % 2], small[:, 48 + n:49 + n], g2b, ALU.mult, ALU.mult).then_inc(t_ready, 1)

                def softmax(part, n):
                    lo, hi = PARTS[part]
                    Lp, sm = L[:, lo:hi, :], smx[:, lo:hi]
                    wide = sm.unsqueeze(2).to_broadcast([P, hi - lo, NE])
                    read_out(dve, ("lg", n))
                    st.do(dve.tensor_reduce(sm, Lp, AX.X, ALU.max))
                    st.settle()
                    dve.tensor_tensor(Lp, Lp, wide, ALU.subtract).then_inc(soft_dve, 1)
                    dve.wait_ge(soft_act, part + 1)
                    st.do(dve.tensor_reduce(sm, Lp, AX.X, ALU.add))
                    st.settle()
                    st.do(dve.reciprocal(sm, sm))
                    st.settle()
                    dve.tensor_tensor(Lp, Lp, wide, ALU.mult).then_inc(aff_ready, 1)

                def rank(part, r0, r1):
                    lo, hi, at = RANGES[part]
                    for r in range(r0, r1):
                        c = slice(at + 8 * r, at + 8 * r + 8)
                        st.do(dve.max(vals[:, c], AF[:, lo:hi]))
                        st.settle()
                        st.do(dve.max_index(inds[:, c], vals[:, c], AF[:, lo:hi]))
                        st.do(dve.match_replace(AF[:, lo:hi], vals[:, c], AF[:, lo:hi], -1.0))
                        st.settle()

                rounds = RANK_S // 8
                spread = {STEP_A + 1: (0, 0, 1, 5), STEP_A + 2: (0, 5, 6, 10), STEP_B: (0, 10, 11, rounds),
                          STEP_B + 1: (1, 0, 2, 6)}
                for n in range(NT):
                    dve.wait_ge(x3_in[n % 2], x3_count(n))
                    if n >= 2:
                        dve.wait_ge(x2_out[n % 2], 16 * (n // 2))
                        dve.wait_ge(t_out[n % 2], 16 * (n // 2))
                        multiplied(dve, ("tT", n - 2, 1))
                    if n == STEP_A + 1:
                        for g in (0, 1):
                            read_out(dve, ("af", g))
                    if n == STEP_B + 1:
                        read_out(dve, ("af", 2))
                    if n in spread:
                        part, r0, r1, r2 = spread[n]
                        rank(part, r0, r1)
                    add(n, 0)
                    if n in spread:
                        rank(part, r1, r2)
                    if n == STEP_A:
                        softmax(0, n - 1)
                    if n == STEP_B:
                        softmax(1, n - 1)
                    add(n, 1)
                    norm(n)
                    if n + 2 < NT and ORDER_B[n + 2] in PADDED:
                        rows = slice(0, 64) if ORDER_B[n + 2] == 0 else slice(64, P)
                        dve.memset(x_t[n % 2][rows, :], 0.0).then_inc(x3_clear, 1)
                rank(1, 6, 8)
                softmax(2, NT - 1)
                rank(1, 8, rounds)
                read_out(dve, ("af", 3))
                rank(2, 0, -(-CAP_P // 8))
                va, vb = vals[:, 0:CAP_S], vals[:, RANK_S:RANK_S + CAP_S][:, ::-1]
                ia, ib = inds[:, 0:CAP_S], inds[:, RANK_S:RANK_S + CAP_S][:, ::-1]
                rows, later, first = ranked[:, 0, 0:CAP_S], merge[:, 0, :], merge[:, 1, :]
                at_p = 2 * RANK_S
                st.do(dve.tensor_tensor(first, va, vb, ALU.is_ge))
                st.do(dve.tensor_tensor(ranked[:, 1, 0:CAP_S], va, vb, ALU.max))
                st.do(dve.tensor_scalar(rows, ia, float(RANGES[0][0]), None, ALU.add))
                st.do(dve.tensor_scalar(later, ib, float(RANGES[1][0]), None, ALU.add))
                st.do(dve.tensor_scalar(ranked[:, 0, CAP_S:SLOTS], inds[:, at_p:at_p + CAP_P], float(RANGES[2][0]), None, ALU.add))
                st.do(dve.tensor_copy(ranked[:, 1, CAP_S:SLOTS], vals[:, at_p:at_p + CAP_P]))
                st.settle()
                st.do(dve.tensor_tensor(rows, rows, later, ALU.subtract))
                st.settle()
                st.do(dve.tensor_tensor(rows, rows, first, ALU.mult))
                st.settle()
                dve.tensor_tensor(rows, rows, later, ALU.add).then_inc(ranked_ready, 1)
                multiplied(dve, ("ix",))
                b = plan[("ix",)][0]
                for blk, n in ((0, P), (1, SB_ROWS)):
                    st.do(dve.tensor_copy(idxc[0:n, blk, :], ps[b][0:n, (2 * blk) * NE:(2 * blk + 1) * NE]))
                    st.do(dve.tensor_copy(gatec[0:n, blk, :], ps[b][0:n, (2 * blk + 1) * NE:(2 * blk + 2) * NE]))
                st.settle()

            @block.tensor
            def _(pe):
                def bank(key):
                    b, k = plan[key]
                    if k > 1:
                        pe.wait_ge(free[b], k - 1)
                    return b

                def transposes(name, n, source):
                    for h in range(2):
                        b = bank((name, n, h))
                        for k in range(4):
                            last = pe.transpose(ps[b][:, k * P:(k + 1) * P], source(4 * h + k), ident[:, :])
                        last.then_inc(full[b], 1)

                def transpose_y(n):
                    pe.wait_ge(y_in[n % 2], 16 * (n // 2 + 1))
                    pe.wait_ge(y_scaled_b, n + 1)
                    own = og[:, ORDER_B[n], :, :].rearrange("p h d -> p (h d)")
                    transposes("yT", n, lambda k: y_t[n % 2][:, k * P:(k + 1) * P] if k * P < Y_W else own[:, k * P - Y_W:(k + 1) * P - Y_W])

                def transpose_t(n):
                    pe.wait_ge(t_ready, n + 1)
                    transposes("tT", n, lambda k: t_t[n % 2][:, k * P:(k + 1) * P])

                def logits(n):
                    if n == 0:
                        pe.wait_ge(wr_in, 16)
                    read_out(pe, ("tT", n, 1))
                    b = bank(("lg", n))
                    for k in range(KT):
                        last = pe.matmul(ps[b][:, 0:NE], tT_t[n % 2][:, k * P:(k + 1) * P], wr[:, k, :], start=k == 0, stop=k == KT - 1)
                    last.then_inc(full[b], 1)

                def project(n, h):
                    b = bank(("wo", n, h))
                    for k in range(KT):
                        last = pe.matmul(ps[b][:, :], yT_t[n % 2][:, k * P:(k + 1) * P], wout[:, k, 512 * h:512 * h + 512],
                                         start=k == 0, stop=k == KT - 1)
                    last.then_inc(full[b], 1)

                def affinities(g):
                    b = bank(("af", g))
                    lo, hi = AF_TILES[g]
                    for i in range(lo, hi):
                        last = pe.transpose(ps[b][0:NE, (i - lo) * P:(i - lo + 1) * P], L[:, i, :], ident[:, :])
                    last.then_inc(full[b], 1)

                transpose_y(0)
                pe.wait_ge(wout_in, 16)
                for n in range(NT):
                    read_out(pe, ("yT", n, 1))
                    project(n, 0)
                    if n:
                        transpose_t(n - 1)
                    if n + 1 < NT:
                        transpose_y(n + 1)
                    if n:
                        logits(n - 1)
                    project(n, 1)
                    if n == STEP_A:
                        pe.wait_ge(aff_ready, 1)
                        affinities(0)
                        affinities(1)
                    if n == STEP_B:
                        pe.wait_ge(aff_ready, 2)
                        affinities(2)
                transpose_t(NT - 1)
                logits(NT - 1)
                pe.wait_ge(aff_ready, 3)
                affinities(3)
                pe.wait_ge(ranked_ready, 1)
                b = bank(("ix",))
                for blk, (lo, hi) in enumerate(((0, P), (P, SLOTS))):
                    for w in range(2):
                        c = (2 * blk + w) * NE
                        last = pe.transpose(ps[b][0:hi - lo, c:c + NE], ranked[:, w, lo:hi], ident[0:NE, 0:NE])
                last.then_inc(full[b], 1)

        xe = arena[:, 0:2 * D].rearrange("p (b n) -> p b n", b=2)
        xeT = arena[:, 2048:2048 + KT * SLOTS].rearrange("p (k s) -> p k s", k=KT)
        hidT = arena[:, 3360:3360 + KT * SLOTS].rearrange("p (k s) -> p k s", k=KT)
        sil = arena[:, 4672:4672 + 4 * SLOTS].rearrange("p (b f s) -> p b f s", b=2, f=2)
        yeT = arena[:, 5328:5328 + KT * SLOTS].rearrange("p (k s) -> p k s", k=KT)
        yeS = arena[:, 6640:6640 + 2 * D].rearrange("p (b n) -> p b n", b=2)
        cur_gather = sb("cur_gather", [P, 2, 1], U32)
        cur_scatter = sb("cur_scatter", [P, 2, 1], U32)
        gu_full, sil_done, hid_done = sem("gu_full"), sem("sil_done"), sem("hid_done")
        dn_full, dn_done = sem("dn_full"), sem("dn_done")
        t_full, t_done = sem("t_full"), sem("t_done")
        o_full, o_done = sem("o_full"), sem("o_done")
        xe_in, acc_out, ye_free, idx_step = sem("xe_in"), sem("acc_out"), sem("ye_free"), sem("idx_step")
        passed, passed_pe = sem("passed"), sem("passed_pe")
        BLKS = ((0, P), (1, SB_ROWS))

        def pair_of_tiles(b):
            return ps[b][:, 0:2 * SLOTS].rearrange("p (f s) -> p f s", f=2)

        with nc.Block() as block:
            @block.sync
            def _(sp):
                with sp.Fori(0, NE - 1) as i:
                    for s in range(6):
                        done = (gu_full, 2) if s < 2 else (gu_full, 4) if s < 4 else (dn_full, 2 * (s - 3))
                        sp.wait_ge(done[0], i * 4 + done[1])
                        sp.dma_start(ring[s], expert_source(s, bass.ds(i + 1, 1))).then_inc(slot_in[s], 16)

            @block.gpsimd
            def _(pool):
                def gather(e, n_steps):
                    at = bass.ds(e, 1)
                    for blk, n in BLKS:
                        pool.tensor_copy(cur_gather[0:n, blk, :], idxc[0:n, blk, at]).then_inc(idx_step, 1)
                    pool.wait_ge(idx_step, n_steps + 2)
                    pool.sem_inc(passed, 1)
                    for blk, n in BLKS:
                        pool.indirect_dma_start(out=xe[0:n, blk, :], out_offset=None, in_=t_d[:, :],
                                                in_offset=bass.IndirectOffsetOnAxis(ap=cur_gather[0:n, blk, :], axis=0)).then_inc(xe_in, 16)

                def scatter(e, n_steps):
                    at = bass.ds(e, 1)
                    for blk, n in BLKS:
                        pool.tensor_copy(cur_scatter[0:n, blk, :], idxc[0:n, blk, at]).then_inc(idx_step, 1)
                    pool.wait_ge(idx_step, n_steps + 2)
                    pool.sem_inc(passed, 1)
                    pool.wait_ge(o_done, e * 4 + 5)
                    pool.sem_inc(passed, 1)
                    for blk, n in BLKS:
                        pool.indirect_dma_start(out=acc_d[:, :], out_offset=bass.IndirectOffsetOnAxis(ap=cur_scatter[0:n, blk, :], axis=0),
                                                in_=yeS[0:n, blk, :], in_offset=None, compute_op=ALU.add).then_inc(acc_out, 16)
                    pool.wait_ge(acc_out, e * 32 + 32)
                    pool.sem_inc(ye_free, 1)

                pool.sem_inc(ye_free, 1)
                gather(0, 0)
                pool.wait_ge(t_full, 4)
                gather(1, 2)
                with pool.Fori(0, NE - 2) as i:
                    pool.wait_ge(t_full, i * 4 + 8)
                    pool.sem_inc(passed, 1)
                    gather(i + 2, i * 4 + 4)
                    scatter(i, i * 4 + 6)
                pool.wait_ge(xe_in, 32 * NE)
                for e in (NE - 2, NE - 1):
                    scatter(e, 2 * NE + 2 * e)

            @block.scalar
            def _(act):
                def silu(e):
                    for fp in range(4):
                        act.wait_ge(gu_full, e * 4 + fp + 1)
                        act.wait_ge(hid_done, e * 4 + fp + 1)
                        act.activation(sil[:, fp % 2, :, :], pair_of_tiles(fp % 2), ACT.Silu).then_inc(sil_done, 1)

                def results(e):
                    for dp in range(4):
                        act.wait_ge(dn_full, e * 4 + dp + 1)
                        act.activation(yeT[:, 2 * dp:2 * dp + 2, :], pair_of_tiles(4 + dp % 2), ACT.Copy).then_inc(dn_done, 1)

                act.sem_inc(dn_done, 2)
                silu(0)
                with act.Fori(0, NE - 1) as i:
                    results(i)
                    silu(i + 1)
                results(NE - 1)

            @block.vector
            def _(dve):
                def move_rows(e):
                    for m in range(4):
                        dve.wait_ge(t_full, e * 4 + m + 1)
                        dve.tensor_copy(xeT[:, 2 * m:2 * m + 2, :], pair_of_tiles(6)).then_inc(t_done, 1)

                def hidden(e, fp):
                    dve.wait_ge(sil_done, e * 4 + fp + 1)
                    dve.tensor_tensor(hidT[:, 2 * fp:2 * fp + 2, :], pair_of_tiles(2 + fp % 2), sil[:, fp % 2, :, :], ALU.mult).then_inc(hid_done, 1)

                def scaled(e, m):
                    h, (blk, n) = m // 2, BLKS[m % 2]
                    if m == 0:
                        dve.wait_ge(ye_free, e + 1)
                    dve.wait_ge(o_full, e * 4 + m + 1)
                    dve.tensor_scalar(yeS[0:n, blk, 512 * h:512 * h + 512], ps[7][0:n, :], gatec[0:n, blk, bass.ds(e, 1)], None,
                                      ALU.mult).then_inc(o_done, 1)

                dve.sem_inc(hid_done, 2)
                dve.sem_inc(o_done, 1)
                move_rows(0)
                for fp in range(4):
                    hidden(0, fp)
                with dve.Fori(0, NE - 1) as i:
                    move_rows(i + 1)
                    for m in range(4):
                        hidden(i + 1, m)
                        scaled(i, m)
                for m in range(4):
                    scaled(NE - 1, m)

            @block.tensor
            def _(pe):
                def transpose_rows(e, m, first=False):
                    if not first:
                        pe.wait_ge(t_done, e * 4 + m)
                    for a in range(2):
                        k = 2 * m + a
                        for (blk, n), c in zip(BLKS, (0, P)):
                            last = pe.transpose(ps[6][:, a * SLOTS + c:a * SLOTS + c + n], xe[0:n, blk, k * P:(k + 1) * P], ident[0:n, 0:n])
                    last.then_inc(t_full, 1)

                def gate_up(e, fp):
                    if fp == 0:
                        pe.wait_ge(t_done, e * 4 + 4)
                    if fp % 2 == 0:
                        for s in (fp, fp + 1):
                            pe.wait_ge(slot_in[s], e * 16 + 16)
                    pe.wait_ge(hid_done, e * 4 + fp + 1)
                    for w in range(2):
                        for a in range(2):
                            f = (2 * fp + a) % 4
                            for k in range(KT):
                                last = pe.matmul(ps[2 * w + fp % 2][:, a * SLOTS:(a + 1) * SLOTS], ring[2 * (fp // 2) + w][:, k, f * P:(f + 1) * P],
                                                 xeT[:, k, :], start=k == 0, stop=k == KT - 1)
                    last.then_inc(gu_full, 1)

                def down(e, dp):
                    if dp % 2 == 0:
                        pe.wait_ge(slot_in[4 + dp // 2], e * 16 + 16)
                    if dp == 0:
                        pe.wait_ge(hid_done, e * 4 + 5)
                    pe.wait_ge(dn_done, e * 4 + dp + 1)
                    for a in range(2):
                        dt = (2 * dp + a) % 4
                        for k in range(KT):
                            if dp == 0 and a == 0 and k == 6:
                                pe.wait_ge(hid_done, e * 4 + 6)
                            last = pe.matmul(ps[4 + dp % 2][:, a * SLOTS:(a + 1) * SLOTS], ring[4 + dp // 2][:, k, dt * P:(dt + 1) * P],
                                             hidT[:, k, :], start=k == 0, stop=k == KT - 1)
                    last.then_inc(dn_full, 1)

                def transpose_results(e, m):
                    h, (blk, n) = m // 2, BLKS[m % 2]
                    pe.wait_ge(dn_done, e * 4 + 2 * h + 4)
                    pe.wait_ge(o_done, e * 4 + m + 1)
                    if blk:
                        pe.sem_inc(passed_pe, 1)
                    for k in range(4):
                        last = pe.transpose(ps[7][0:n, k * P:(k + 1) * P], yeT[:, 4 * h + k, blk * P:blk * P + n], ident[:, :])
                    last.then_inc(o_full, 1)

                pe.wait_ge(xe_in, 32)
                for m in range(4):
                    transpose_rows(0, m, first=m == 0)
                for fp in range(4):
                    gate_up(0, fp)
                with pe.Fori(0, NE - 1) as i:
                    pe.wait_ge(xe_in, i * 32 + 64)
                    for m in range(4):
                        transpose_rows(i + 1, m)
                        down(i, m)
                    for m in range(4):
                        gate_up(i + 1, m)
                        transpose_results(i, m)
                for m in range(4):
                    down(NE - 1, m)
                    if m == 2:
                        transpose_results(NE - 1, 0)
                        transpose_results(NE - 1, 1)
                for m in (2, 3):
                    transpose_results(NE - 1, m)

        fin = [arena[:, 11 * D + i * D:12 * D + i * D] for i in range(NT)]
        fgb = arena[:, 22 * D:23 * D]
        fin_in = [sem(f"fin{i}_in") for i in range(NT)]
        fg_in, fin_sq, fin_ready, y_stored = sem("fg_in"), sem("fin_sq"), sem("fin_ready"), sem("y_stored")
        outs = {0: [(64, y_prompt[0, 0:64, :])], 1: [(0, y_prompt[0, 64:192, :])], 2: [(0, y_prompt[0, 192:256, :])]}
        for i in range(3, NT):
            outs[i] = [(0, y_sample[0, (i - 3) * P:(i - 2) * P, :])]
        with nc.Block() as block:
            @block.sync
            def _(sp):
                sp.dma_start(fgb, final_g.rearrange("(a n) -> a n", a=1).to_broadcast([P, D])).then_inc(fg_in, 16)
                for i in range(NT):
                    sp.dma_start(fin[i], acc_d[i * P:(i + 1) * P, :]).then_inc(fin_in[i], 16)
                for i in range(NT):
                    sp.wait_ge(fin_ready, i + 1)
                    for p0, dst in outs[i]:
                        sp.dma_start(dst, fin[i][p0:p0 + dst.shape[0], :]).then_inc(y_stored, 16)
                sp.wait_ge(y_stored, 16 * NT)

            @block.scalar
            def _(act):
                st = Steps(act, sem("act_step_d"))
                for i in range(NT):
                    act.wait_ge(fin_in[i], 16)
                    if i:
                        st.settle()
                    st.do(act.activation(junk_b, fin[i], ACT.Square, accum_out=small[:, i:i + 1]))
                    st.settle()
                    act.activation(small[:, 32 + i:33 + i], small[:, i:i + 1], ACT.Sqrt, scale=1.0 / D, bias=small[:, 94:95]).then_inc(fin_sq, 1)

            @block.vector
            def _(dve):
                st = Steps(dve, sem("dve_step_d"))
                dve.wait_ge(fg_in, 16)
                for i in range(NT):
                    dve.wait_ge(fin_sq, i + 1)
                    st.do(dve.reciprocal(small[:, 48 + i:49 + i], small[:, 32 + i:33 + i]))
                    st.settle()
                    dve.scalar_tensor_tensor(fin[i], fin[i], small[:, 48 + i:49 + i], fgb, ALU.mult, ALU.mult).then_inc(fin_ready, 1)


_INS = ("x_prompt", "x_sample", "meta_tokens", "norm1_g", "w_in", "conv_w", "conv_b", "gate_b", "pool_w", "pool_scale",
        "mh_norm_g", "w_out", "norm2_g", "w_router", "w_gate", "w_up", "w_down", "final_g")


def window_reciprocals():
    out = np.ones((4, T), np.float32)
    for g, w in enumerate((2, 4, 8, 16)):
        for lo, hi in REAL:
            t = np.arange(hi - lo)
            n = np.clip(t - w // 2 + w, 0, hi - lo) - np.clip(t - w // 2, 0, hi - lo)
            out[g, lo:hi] = np.float32(1.0) / n.astype(np.float32)
    return out


def kernel(**inputs):
    import concourse.bacc as bacc
    from concourse.bass_utils import run_bass_kernel_spmd

    nc = bacc.Bacc("TRN2", target_bir_lowering=False, num_devices=1)
    arrays = {f"in_{n}": np.ascontiguousarray(inputs[n]) for n in _INS}
    arrays["window_reciprocals"] = window_reciprocals()
    args = [nc.dram_tensor(n, a.shape, mybir.dt.from_np(a.dtype), kind="ExternalInput").ap() for n, a in arrays.items()]
    outs = [nc.dram_tensor(n, (1, rows, D), F32, kind="ExternalOutput").ap()
            for n, rows in (("y_prompt", SEQ_P), ("y_sample", SEQ_S))]
    encoder_program(nc, *args, *outs)
    r = run_bass_kernel_spmd(nc, [arrays], core_ids=[0])
    return r.results[0]["y_prompt"], r.results[0]["y_sample"]
```
